# Optimizing a Trainium2 kernel written in Bass

```python
import jax, jax.numpy as jnp
from jax import lax
import numpy as np

D_MODEL = 1024
BATCH = 1
SEQ = 256
DEPTH = 1

CONV_WIDTH = D_MODEL
CONV_K = 3
RWKV_HEAD = 64
RWKV_HEADS = D_MODEL // RWKV_HEAD
RWKV_WIDTH = RWKV_HEADS * RWKV_HEAD
DECAY_LORA = 64
AAA_LORA = 64
GATE_LORA = 160
N_EXPERTS = 32
TOP_K = 4
D_FF = D_MODEL
SWIGLU_ALPHA = 1.702
SWIGLU_LIMIT = 7.0
MOE_BLOCK = 256
NORM_EPS = 1e-5
GN_EPS = 64e-5
CONV_COLS = 3 * CONV_WIDTH
RWKV_COLS = 3 * RWKV_WIDTH + DECAY_LORA + AAA_LORA + GATE_LORA
GATE_COLS = 2 * D_MODEL
PROJ_COLS = CONV_COLS + RWKV_COLS + GATE_COLS

kernel_name = "hybrid_conv_rwkv7_moe_block"

def rmsnorm(x, g):
    xf = x.astype(jnp.float32)
    y = xf * lax.rsqrt(jnp.mean(xf * xf, axis=-1, keepdims=True) + NORM_EPS)
    return (y * g.astype(jnp.float32)).astype(x.dtype)

def short_conv_mixer(p, conv_w):
    gb, gc, xin = jnp.split(p, 3, axis=-1)
    u = gc * xin
    s = u.shape[1]
    up = jnp.pad(u, ((0, 0), (CONV_K - 1, 0), (0, 0)))
    conv = sum(conv_w[j] * up[:, j:j + s] for j in range(CONV_K))
    return gb * conv

def rwkv7_time_mix(p, mu, w0, w2, a0, a2, g2, k_k, k_a, r_k, ln_g, ln_b):
    f32 = jnp.float32
    bsz, s, _ = p.shape
    p = p.astype(f32)
    p_prev = jnp.pad(p, ((0, 0), (1, 0), (0, 0)))[:, :-1]
    p = p + (p_prev - p) * mu
    r, k, v, wd, ad, gd = jnp.split(
        p, [RWKV_WIDTH, 2 * RWKV_WIDTH, 3 * RWKV_WIDTH,
            3 * RWKV_WIDTH + DECAY_LORA, 3 * RWKV_WIDTH + DECAY_LORA + AAA_LORA], axis=-1)
    w = -jax.nn.softplus(-(w0 + jnp.tanh(wd) @ w2)) - 0.5
    decay = jnp.exp(-jnp.exp(w))
    a = jax.nn.sigmoid(a0 + ad @ a2)
    g = jax.nn.sigmoid(gd) @ g2
    heads = lambda t: t.reshape(bsz, s, RWKV_HEADS, RWKV_HEAD)
    kk = heads(k * k_k)
    kk = kk / jnp.maximum(jnp.sqrt(jnp.sum(kk * kk, axis=-1, keepdims=True)), 1e-12)
    k = k * (1.0 + (a - 1.0) * k_a)
    r_h, k_h, v_h, w_h, a_h = heads(r), heads(k), heads(v), heads(decay), heads(a)

    def step(state, inp):
        r_t, w_t, k_t, v_t, kk_t, a_t = inp
        sa = jnp.einsum('bhij,bhj->bhi', state, kk_t)
        state = (state * w_t[:, :, None, :]
                 + jnp.einsum('bhi,bhj->bhij', -sa, kk_t * a_t)
                 + jnp.einsum('bhi,bhj->bhij', v_t, k_t))
        return state, jnp.einsum('bhij,bhj->bhi', state, r_t)

    xs = tuple(jnp.moveaxis(t, 1, 0) for t in (r_h, w_h, k_h, v_h, kk, a_h))
    s0 = jnp.zeros((bsz, RWKV_HEADS, RWKV_HEAD, RWKV_HEAD), f32)
    _, y = lax.scan(step, s0, xs)
    y = jnp.moveaxis(y, 0, 1)
    mean = jnp.mean(y, axis=-1, keepdims=True)
    var = jnp.mean(jnp.square(y - mean), axis=-1, keepdims=True)
    y = ((y - mean) * lax.rsqrt(var + GN_EPS)).reshape(bsz, s, RWKV_WIDTH) * ln_g + ln_b
    bonus = (jnp.sum(r_h * k_h * r_k, axis=-1, keepdims=True) * v_h).reshape(bsz, s, RWKV_WIDTH)
    return (y + bonus) * g

def clamped_swiglu(u):
    glu, lin = jnp.split(u, 2, axis=-1)
    glu = jnp.minimum(glu, SWIGLU_LIMIT)
    lin = jnp.clip(lin, -SWIGLU_LIMIT, SWIGLU_LIMIT)
    return glu * jax.nn.sigmoid(SWIGLU_ALPHA * glu) * (lin + 1.0)

def moe_ffn(h, router_w, router_b, w1, b1, w2, b2):
    t, d = h.shape
    logits = (h @ router_w + router_b).astype(jnp.float32)
    top_val, top_idx = lax.top_k(logits, TOP_K)
    gates = jax.nn.softmax(top_val, axis=-1).astype(h.dtype)
    n_assign = t * TOP_K
    flat_e = top_idx.reshape(-1)
    order = jnp.argsort(flat_e)
    sorted_e = flat_e[order]
    counts = jnp.bincount(flat_e, length=N_EXPERTS).astype(jnp.int32)
    padded = (counts + MOE_BLOCK - 1) // MOE_BLOCK * MOE_BLOCK
    start = jnp.cumsum(counts) - counts
    padded_end = jnp.cumsum(padded)
    padded_start = padded_end - padded
    slot_sorted = (padded_start[sorted_e] + jnp.arange(n_assign, dtype=jnp.int32) - start[sorted_e]).astype(jnp.int32)
    slot = jnp.zeros((n_assign,), jnp.int32).at[order].set(slot_sorted)
    n_blocks = -(-n_assign // MOE_BLOCK) + N_EXPERTS
    n_slots = n_blocks * MOE_BLOCK
    slot_token = jnp.full((n_slots,), t, jnp.int32).at[slot].set(
        jnp.arange(n_assign, dtype=jnp.int32) // TOP_K)
    block_expert = jnp.minimum(
        jnp.searchsorted(padded_end, jnp.arange(n_blocks, dtype=jnp.int32) * MOE_BLOCK, side='right'),
        N_EXPERTS - 1)
    h_pad = jnp.concatenate([h, jnp.zeros((1, d), h.dtype)], axis=0)
    xb = h_pad[slot_token].reshape(n_blocks, MOE_BLOCK, d)

    def expert_block(args):
        xblk, e = args
        u = xblk @ w1[e] + b1[e]
        return clamped_swiglu(u) @ w2[e] + b2[e]

    yb = lax.map(expert_block, (xb, block_expert)).reshape(n_slots, d)
    return jnp.einsum('tkd,tk->td', yb[slot].reshape(t, TOP_K, d), gates)

def setup_inputs(seed: int = 0) -> dict:
    key = jax.random.key(seed)
    ks = jax.random.split(key, 24)
    L = DEPTH
    nrm = lambda k, shape, scale: jax.random.normal(k, shape, jnp.float32) * scale
    return {
        "x": nrm(ks[0], (BATCH, SEQ, D_MODEL), 1.0),
        "norm_mix_g": 1.0 + nrm(ks[1], (L, D_MODEL), 0.02),
        "w_in": nrm(ks[2], (L, D_MODEL, PROJ_COLS), D_MODEL ** -0.5),
        "conv_w": nrm(ks[3], (L, CONV_K, CONV_WIDTH), CONV_K ** -0.5),
        "shift_mu": jax.random.uniform(ks[4], (L, RWKV_COLS), jnp.float32),
        "decay_w0": jax.random.uniform(ks[5], (L, RWKV_WIDTH), jnp.float32, minval=-6.0, maxval=-1.0),
        "decay_w2": nrm(ks[6], (L, DECAY_LORA, RWKV_WIDTH), 0.1 * DECAY_LORA ** -0.5),
        "iclr_a0": nrm(ks[7], (L, RWKV_WIDTH), 0.5),
        "iclr_a2": nrm(ks[8], (L, AAA_LORA, RWKV_WIDTH), 0.1 * AAA_LORA ** -0.5),
        "gate_g2": nrm(ks[9], (L, GATE_LORA, RWKV_WIDTH), GATE_LORA ** -0.5),
        "k_k": 0.85 + nrm(ks[10], (L, RWKV_WIDTH), 0.02),
        "k_a": 1.0 + nrm(ks[11], (L, RWKV_WIDTH), 0.02),
        "r_k": nrm(ks[12], (L, RWKV_HEADS, RWKV_HEAD), 0.1),
        "ln_x_g": 1.0 + nrm(ks[13], (L, RWKV_WIDTH), 0.02),
        "ln_x_b": nrm(ks[14], (L, RWKV_WIDTH), 0.01),
        "w_out": nrm(ks[15], (L, D_MODEL, D_MODEL), D_MODEL ** -0.5),
        "norm_ffn_g": 1.0 + nrm(ks[16], (L, D_MODEL), 0.02),
        "router_w": nrm(ks[17], (L, D_MODEL, N_EXPERTS), D_MODEL ** -0.5),
        "router_b": nrm(ks[18], (L, N_EXPERTS), 0.01),
        "exp_w1": nrm(ks[19], (L, N_EXPERTS, D_MODEL, 2 * D_FF), D_MODEL ** -0.5),
        "exp_b1": nrm(ks[20], (L, N_EXPERTS, 2 * D_FF), 0.01),
        "exp_w2": nrm(ks[21], (L, N_EXPERTS, D_FF, D_MODEL), D_FF ** -0.5),
        "exp_b2": nrm(ks[22], (L, N_EXPERTS, D_MODEL), 0.01),
        "norm_final_g": 1.0 + nrm(ks[23], (D_MODEL,), 0.02),
    }

def reference(x, norm_mix_g, w_in, conv_w, shift_mu, decay_w0, decay_w2, iclr_a0, iclr_a2,
              gate_g2, k_k, k_a, r_k, ln_x_g, ln_x_b, w_out, norm_ffn_g, router_w, router_b,
              exp_w1, exp_b1, exp_w2, exp_b2, norm_final_g):
    bsz, s, d = x.shape
    h = x
    for l in range(DEPTH):
        xn = rmsnorm(h, norm_mix_g[l])
        p = xn @ w_in[l]
        p_conv, p_rwkv, p_gate = jnp.split(p, [CONV_COLS, CONV_COLS + RWKV_COLS], axis=-1)
        y_conv = short_conv_mixer(p_conv, conv_w[l])
        y_rwkv = rwkv7_time_mix(p_rwkv, shift_mu[l], decay_w0[l], decay_w2[l], iclr_a0[l],
                                iclr_a2[l], gate_g2[l], k_k[l], k_a[l], r_k[l],
                                ln_x_g[l], ln_x_b[l]).astype(h.dtype)
        gate_conv, gate_rwkv = jnp.split(jax.nn.sigmoid(p_gate), 2, axis=-1)
        h = h + (gate_conv * y_conv + gate_rwkv * y_rwkv) @ w_out[l]
        hn = rmsnorm(h, norm_ffn_g[l]).reshape(bsz * s, d)
        h = h + moe_ffn(hn, router_w[l], router_b[l], exp_w1[l], exp_b1[l],
                        exp_w2[l], exp_b2[l]).reshape(bsz, s, d)
    return rmsnorm(h, norm_final_g)


_drawn_inputs = setup_inputs


def setup_inputs(seed=0):
    import zlib

    import numpy as np

    out = dict(_drawn_inputs(seed))
    spreads = {}
    factors = {'decay_w2': 8.0,
     'k_k': 3.589,
     'k_a': 4.402,
     'ln_x_g': 3.316,
     'ln_x_b': 5.148,
     'exp_b1': 8.0,
     'exp_b2': 8.0,
     'norm_final_g': 2.9}
    for name, (base, spread) in spreads.items():
        noise = np.random.default_rng([zlib.crc32(name.encode()), seed]).standard_normal(out[name].shape)
        drawn = base * np.exp(spread * noise) if base else spread * noise
        out[name] = __import__('jax').numpy.asarray(drawn.astype(out[name].dtype))
    for name, factor in factors.items():
        out[name] = (out[name] * factor).astype(out[name].dtype)
    return out
```

```python
from contextlib import ExitStack

import numpy as np

import concourse.bass as bass
from concourse import mybir

ALU = mybir.AluOpType
ACT = mybir.ActivationFunctionType
F32 = mybir.dt.float32
BF16 = mybir.dt.bfloat16
I32 = mybir.dt.int32
U32 = mybir.dt.uint32
AX_X = mybir.AxisListType.X

P = 128
T = 256
D = 1024
TT = T // P
KT = D // P
HEAD = 64
E = 32
TOP = 4
CAP = 64
NORM_EPS, GN_EPS = 1e-5, 64e-5
ALPHA, LIMIT = 1.702, 7.0
KAPPA = float(np.exp(-0.5))
FAR = 1.0e4

COL_GB, COL_GC, COL_XIN = 0, D, 2 * D
COL_R, COL_K, COL_V = 3 * D, 4 * D, 5 * D
COL_LORA = 6 * D
LORA = 288
COL_GATE_CONV = COL_LORA + LORA
COL_GATE_RWKV = COL_GATE_CONV + D
CHUNK = 512

CONSTS = ["ident", "above", "above_eq", "below", "below16", "above16", "pair16", "pair32", "pair64",
          "head_ones", "ones", "slot", "expert", "pick"]
C_AT = {n: i * P for i, n in enumerate(CONSTS)}

PARAMS = [("norm_mix_g", 8), ("mu_r", 8), ("mu_k", 8), ("mu_v", 8), ("mu_lora", 3), ("w0", 8), ("a0", 8),
          ("k_k", 8), ("k_a", 8), ("r_k", 8), ("ln_g", 8), ("ln_b", 8), ("conv0", 8), ("conv1", 8), ("conv2", 8)]
P_AT, _n = {}, 0
for _name, _w in PARAMS:
    P_AT[_name] = _n
    _n += _w
NPAR = _n


def constants():
    p, f = np.arange(P)[:, None], np.arange(P)[None, :]
    pair = lambda b: (p // (2 * b) == f // (2 * b)) & (p // b % 2 == 0) & (f // b % 2 == 1)
    same16 = p // 16 == f // 16
    m = {
        "ident": p == f, "above": f > p, "above_eq": f >= p, "below": f < p,
        "below16": (f < p) & same16, "above16": (f > p) & same16,
        "pair16": pair(16), "pair32": pair(32), "pair64": pair(64),
        "head_ones": p // HEAD == f // HEAD, "ones": p == p + 0 * f,
        "slot": f % CAP + 0 * p, "expert": f % E + 0 * p, "pick": (p % E == f) & (p < 3 * E),
    }
    return np.concatenate([np.asarray(m[n], np.float32) for n in CONSTS], axis=1)


def build(nc, x, w_in, w_out, norm_ffn_g, norm_final_g, w2, a2, g2, router_w, router_b,
          exp_w1, exp_b1, exp_w2, exp_b2, params, consts, out):
    with ExitStack() as ctx:
        def sb(name, shape, dt=F32):
            return ctx.enter_context(nc.sbuf_tensor(name, shape, dt))

        def sem(name):
            return ctx.enter_context(nc.semaphore(name))

        ring = sb("ring", [P, 12, 2048])
        work = sb("work", [P, 10, 2048])
        arr = lambda t: t.rearrange("p (m t) -> p m t", m=KT)
        Kt, KK, AA, R, V, G1 = (arr(ring[:, 6 + i]) for i in range(6))
        XN, CS, TMP, GC, GB, SW, XI, BON, G, G2 = (arr(work[:, i]) for i in range(10))
        flat = lambda i: work[:, i]
        i_XN, i_CS, i_TMP, i_GC, i_GB, i_SW, i_XI, i_BON, i_G, i_G2 = range(10)
        Y = SW
        cst = sb("cst", [P, len(CONSTS) * P])
        par = sb("par", [P, NPAR])
        inv = sb("inv", [P, 35])
        col = sb("col", [P, 64])
        vtok = sb("vtok", [P, TT, D])
        btok = sb("btok", [P, D])
        ktok = sb("ktok", [P, D])
        zb = sb("zb", [P, 2, 4 * HEAD])
        ub = sb("ub", [P, 2, 4 * HEAD])
        st = sb("st", [P, KT, HEAD])
        cm = sb("cm", [P, KT, 2])
        ce = sb("ce", [P, KT, 2])
        dec = sb("dec", [P, KT])
        C = lambda n, w=P: cst[:, C_AT[n]:C_AT[n] + w]
        pc = lambda n, m, h=P: par[0:h, P_AT[n] + m:P_AT[n] + m + 1]
        ps = [ctx.enter_context(nc.psum_tensor(f"ps{i}", [P, 512], F32)) for i in range(8)]

        ubuf = lambda i, half: flat(i)[:, 1024 * half:1024 * half + 1024].rearrange("p (l n) -> p l n", l=2)
        mL, mA, mAT, mAK = ubuf(i_XN, 0), ubuf(i_XN, 1), ubuf(i_CS, 0), ubuf(i_CS, 1)
        mRK, mRB, mP, mPT = ubuf(i_TMP, 0), ubuf(i_TMP, 1), ubuf(i_GC, 0), ubuf(i_GC, 1)
        mE = ubuf(i_GB, 0)

        const_in = sem("const_in")
        x_in = sem("x_in")
        lora_in = sem("lora_in")
        slot_in = [sem(f"slot_in{i}") for i in range(12)]
        xres_in = sem("xres_in")
        late_in = sem("late_in")
        expert_in = [sem(f"expert_in{i}") for i in range(12)]
        merged = sem("merged")
        dve_chain = sem("dve_chain")
        act_chain = sem("act_chain")
        act_rms = sem("act_rms")
        dve_rms = sem("dve_rms")
        xt_ready = sem("xt_ready")
        xn_ready = sem("xn_ready")
        blk_done = sem("blk_done")
        blk_scaled = sem("blk_scaled")
        blk_shifted = sem("blk_shifted")
        blk_copied = sem("blk_copied")
        lora_act = sem("lora_act")
        dve_step = sem("dve_step")
        pe_sum = sem("pe_sum")
        act_step = sem("act_step")
        pe_tok = sem("pe_tok")
        act_tok = sem("act_tok")
        pe_l = [sem(f"pe_l{i}") for i in range(2)]
        dve_l = [sem(f"dve_l{i}") for i in range(2)]
        act_l = [sem(f"act_l{i}") for i in range(2)]
        wout_done = sem("wout_done")
        xt_done = sem("xt_done")
        dve_h = sem("dve_h")
        act_h = sem("act_h")
        pe_h = sem("pe_h")
        rounds_in = sem("rounds_in")
        sel_ready = sem("sel_ready")
        gathered = sem("gathered")
        gate_turned = sem("gate_turned")
        xe_ready = sem("xe_ready")
        gt_ready = sem("gt_ready")
        b1_used = sem("b1_used")
        w_used = sem("w_used")
        u_free = sem("u_free")
        glu_ready = sem("glu_ready")
        sig_ready = sem("sig_ready")
        act_ready = sem("act_ready")
        act_turned = sem("act_turned")
        at_ready = sem("at_ready")
        y_ready = sem("y_ready")
        combined = sem("combined")
        out_ready = sem("out_ready")
        out_done = sem("out_done")
        lin_ready = sem("lin_ready")
        round_ready = sem("round_ready")

        stream = [(w_in, COL_LORA, LORA)]
        for c0 in (COL_K, COL_R, COL_V, COL_GC, COL_XIN, COL_GB, COL_GATE_CONV, COL_GATE_RWKV):
            stream += [(w_in, c0, CHUNK), (w_in, c0 + CHUNK, CHUNK)]
        NIN = len(stream)
        stream += [(w_out, 0, CHUNK), (w_out, CHUNK, CHUNK)]

        def chunk(n):
            s = 2 * (n % 3)
            return ring[:, s:s + 2, :].rearrange("p s c -> p (s c)").rearrange("p (k c) -> p k c", k=KT)

        def chunk_in(n):
            return slot_in[2 * (n % 3)], 16 * (n // 3 + 1)

        blocks = [(0, 0, P), (0, P, P), (0, 2 * P, 32)]
        for n in range(1, NIN):
            blocks += [(n, i * P, P) for i in range(CHUNK // P)]
        N_SHIFT = 27

        def blocks_until(n):
            last = max(i for i, blk in enumerate(blocks) if blk[0] == n)
            return last + 1 + (3 * KT if last >= N_SHIFT else 0)

        NPE, ND, NA = (22, 21), (17, 16), 11

        def flat_ring(i):
            return ring[:, i]

        def shifted(b):
            n, _, h = blocks[b]
            if b < 3:
                return CS[0:h, b, :]
            return (Kt, R, V)[(b - 3) // 8][:, (b - 3) % 8, :]

        HB = flat(i_XN).rearrange("p (t d) -> p t d", t=TT)
        HN = flat(i_CS).rearrange("p (t d) -> p t d", t=TT)
        HNT = arr(flat(i_TMP))
        H3 = work[:, i_GC:i_GC + 2].rearrange("p a n -> p (a n)")[:, 0:3072].bitcast(BF16).rearrange(
            "p (t s d) -> p t s d", t=TT, s=3)
        h3tmp = flat(i_GB)[:, 1024:2048]
        b1f = flat(i_BON)
        b1s = flat(i_G)[:, 0:1024].bitcast(BF16)
        b2s = flat(i_G)[:, 1024:2048]
        gffn = flat(i_G2)[:, 0:1024]
        gfin = flat(i_G2)[:, 1024:2048]
        xe, glu, sig, lin = (flat(i_XI)[:, 512 * i:512 * i + 512] for i in range(4))
        actb, actT, yb, gts = (flat(i_SW)[:, 512 * i:512 * i + 512] for i in range(4))
        late = vtok[:].rearrange("p c d -> p (c d)")
        rw = late[:, 0:KT * E].rearrange("p (k e) -> p k e", k=KT)
        rb = late[:, 256:256 + E]
        lg = late[:, 320:320 + TT * E].rearrange("p (t e) -> p t e", t=TT)
        mx = sb("mx", [P, TT, 8])
        mi = sb("mi", [P, TT, 8], U32)
        mif = sb("mif", [P, TT, 8])
        ge = sb("ge", [P, TT, 8])
        gw = sb("gw", [P, TT, E])
        msk = sb("msk", [P, TT, E])
        rk = sb("rk", [P, TT, E])
        gwT = late[0:E, 512:512 + T]
        cnt = sb("cnt", [P, 8])
        rounds = sb("rounds", [P, 1], I32)
        sel = sb("sel", [P, TT, CAP], BF16)
        gsel = ktok[:, 0:T].rearrange("p (t n) -> p t n", t=TT)
        oh = sb("oh", [3 * E, CAP], BF16)
        b1m = btok[0:3 * E, :].bitcast(BF16)

        block = ctx.enter_context(nc.Block())

        @block.sync
        def _(sp):
            sp.dma_start(cst[:], consts).then_inc(const_in, 16)
            sp.dma_start(par[:], params).then_inc(const_in, 16)
            sp.dma_start(flat(i_G2).rearrange("p (t d) -> p t d", t=TT),
                         x[0].rearrange("(t p) d -> p t d", p=P)).then_inc(x_in, 16)
            sp.dma_start(flat(i_GB)[0:64, 0:D], w2[0]).then_inc(lora_in, 16)
            sp.dma_start(flat(i_GB)[64:128, 0:D], a2[0]).then_inc(lora_in, 16)
            sp.dma_start(flat(i_GB)[:, D:2 * D], g2[0, 0:P]).then_inc(lora_in, 16)
            sp.dma_start(flat(i_XI)[0:32, 0:D], g2[0, P:P + 32]).then_inc(lora_in, 16)
            for n, (w, c0, width) in enumerate(stream):
                if n >= 3:
                    sp.wait_ge(blk_done, blocks_until(n - 3))
                s, _ = chunk_in(n)
                sp.dma_start(chunk(n)[:, :, 0:width],
                             w[0].rearrange("(k p) n -> p k n", p=P)[:, :, c0:c0 + width]).then_inc(s, 16)
            sp.wait_ge(merged, 1)
            sp.dma_start(HB, x[0].rearrange("(t p) d -> p t d", p=P)).then_inc(xres_in, 16)
            sp.dma_start(rw, router_w[0].rearrange("(k p) e -> p k e", p=P)).then_inc(late_in, 16)
            sp.dma_start(rb, router_b[0:1, :].partition_broadcast(P)).then_inc(late_in, 16)
            for s in range(3):
                sp.dma_start(b1f[E * s:E * s + E, :], exp_b1[0]).then_inc(late_in, 16)
            sp.dma_start(b2s[0:E, :], exp_b2[0]).then_inc(late_in, 16)
            sp.dma_start(gffn, norm_ffn_g[0:1, :].partition_broadcast(P)).then_inc(late_in, 16)
            sp.dma_start(gfin, norm_final_g.partition_broadcast(P)).then_inc(late_in, 16)
            sp.wait_ge(wout_done, 2)
            sp.wait_ge(rounds_in, 1)
            n_rounds = sp.value_load(rounds[0:1, 0:1], min_val=1, max_val=4)
            with sp.Fori(0, n_rounds) as r:
                with sp.Fori(0, E) as e:
                    for j in range(12):
                        sp.wait_ge(w_used, (r * E + e) * 12 + j + 1)
                        if j < 8:
                            src = exp_w1[0, bass.ds(e, 1), j * P:(j + 1) * P, :].rearrange("a p n -> p (a n)")
                            dst = ring[:, j, :]
                        else:
                            src = exp_w2[0, bass.ds(e, 1), (j - 8) * 2 * P:(j - 7) * 2 * P, :].rearrange(
                                "a (s p) n -> p (a s) n", p=P)
                            dst = ring[:, j, :].rearrange("p (s n) -> p s n", s=2)
                        sp.dma_start(dst, src).then_inc(expert_in[j], 16)
            sp.wait_ge(out_ready, 1)
            sp.dma_start(out[0].rearrange("(t p) d -> p t d", p=P), HB).then_inc(out_done, 16)
            sp.wait_ge(out_done, 16)

        @block.tensor
        def _(pe):
            mm = nc.tensor.matmul

            pe.wait_ge(const_in, 32)
            pe.wait_ge(xt_ready, 2)
            xs = ring[:, 11]
            for k in range(KT):
                if k >= 4:
                    pe.wait_ge(xn_ready, k - 3)
                for t in range(TT):
                    last = nc.tensor.transpose(ps[k % 4][:, t * P:(t + 1) * P],
                                               xs[:, t * D + k * P:t * D + (k + 1) * P], C("ident"))
                last.then_inc(xt_done, 1)

            def bank_free(b):
                if b < 4:
                    pe.wait_ge(xn_ready, KT)
                elif b - 4 < N_SHIFT:
                    pe.wait_ge(blk_shifted, b - 3)
                else:
                    pe.wait_ge(blk_copied, b - 3 - N_SHIFT)

            def project(b, n, c0, width):
                bank_free(b)
                s, v = chunk_in(n)
                pe.wait_ge(s, v)
                for k in range(KT):
                    last = mm(ps[b % 4][0:width, 0:T], chunk(n)[:, k, c0:c0 + width], XN[:, k, :],
                              start=k == 0, stop=k == KT - 1)
                last.then_inc(blk_done, 1)

            def head_sums(src, banks):
                for i, b in enumerate(banks):
                    last = mm(ps[b][:, :], C("head_ones"), src[:, 512 * i:512 * i + 512], start=True, stop=True)
                last.then_inc(pe_sum, 1)

            for b in range(N_SHIFT):
                n, c0, width = blocks[b]
                project(b, n, c0, width)
            pe.wait_ge(lora_in, 64)
            pe.wait_ge(lora_act, 3)
            b = N_SHIFT
            for kind in range(3):
                for m in range(KT):
                    bank_free(b)
                    o, cs = ps[b % 4][:, 0:T], slice(m * P, (m + 1) * P)
                    if kind == 0:
                        last = mm(o, flat(i_GB)[0:64, cs], CS[0:64, 0, :], start=True, stop=True)
                    elif kind == 1:
                        last = mm(o, flat(i_GB)[64:128, cs], CS[64:128, 0, :], start=True, stop=True)
                    else:
                        mm(o, flat(i_GB)[:, D + m * P:D + (m + 1) * P], CS[:, 1, :], start=True, stop=False)
                        last = mm(o, flat(i_XI)[0:32, cs], CS[0:32, 2, :], start=False, stop=True)
                    last.then_inc(blk_done, 1)
                    b += 1
            for i in range(N_SHIFT, len(blocks)):
                n, c0, width = blocks[i]
                project(b, n, c0, width)
                b += 1
                if i == N_SHIFT + 7:
                    pe.wait_ge(dve_step, 1)
                    head_sums(flat(i_TMP), (4, 5, 6, 7))
                if i == N_SHIFT + 23:
                    pe.wait_ge(dve_step, 4)
                    head_sums(flat(i_BON), (4, 5, 6, 7))

            pe.wait_ge(dve_step, 5)
            pe.wait_ge(blk_copied, len(blocks) + 24 - N_SHIFT)
            for g, (src, c) in enumerate([(V, 0), (V, 1), (AA, 0), (Kt, 0)]):
                for half in range(2):
                    for i in range(4):
                        last = nc.tensor.transpose(ps[2 * g + half][:, i * P:(i + 1) * P],
                                                   src[:, 4 * half + i, c * P:(c + 1) * P], C("ident"))
                    last.then_inc(pe_tok, 1)
            pe.wait_ge(act_tok, 8)

            U4 = lambda t, i: t[:, i * P:(i + 1) * P]
            Q4 = lambda t, i: t[:, i * HEAD:(i + 1) * HEAD]
            for bt in range(4):
                q, m0 = bt // 2, 4 * (bt % 2)
                rows = slice(64 * q, 64 * q + 64)
                tok = lambda c: slice(c * P, (c + 1) * P)
                hcol = lambda i: slice((m0 + i) * P + 64 * q, (m0 + i) * P + 64 * q + 64)

                def four(c, bank, lhs, rhs, n=P, rows_out=slice(0, P)):
                    for i in range(4):
                        last = mm(ps[4 * c + bank][rows_out, i * n:(i + 1) * n], lhs(i), rhs(i), start=True, stop=True)
                    return last

                f = lambda arr_, c: (lambda i: arr_[rows, m0 + i, tok(c)])
                u = lambda arr_, c: (lambda i: U4(arr_[:, c, :], i))
                for c in range(2):
                    if bt:
                        pe.wait_ge(dve_l[c], bt * ND[c])
                        pe.wait_ge(act_l[c], bt * NA)
                    four(c, 0, f(AA, c), f(KK, c))
                    four(c, 1, f(KK, c), f(AA, c)).then_inc(pe_l[c], 1)
                for c in range(2):
                    four(c, 2, f(Kt, c), f(KK, c))
                    four(c, 3, f(Kt, c), f(R, c)).then_inc(pe_l[c], 1)
                for c in range(2):
                    pe.wait_ge(dve_l[c], bt * ND[c] + 1)
                    four(c, 0, f(AA, c), f(R, c)).then_inc(pe_l[c], 1)
                for c in range(2):
                    pe.wait_ge(dve_l[c], bt * ND[c] + 5)
                    four(c, 1, u(mAT, c), u(mA, c))
                    four(c, 2, u(mA, c), u(mAT, c)).then_inc(pe_l[c], 1)
                for c in range(2):
                    pe.wait_ge(act_l[c], bt * NA + 1)
                    pe.wait_ge(dve_l[c], bt * ND[c] + 6)
                    four(c, 3, u(mP, c), u(mE, c)).then_inc(pe_l[c], 1)
                for c in range(2):
                    pe.wait_ge(act_l[c], bt * NA + 2)
                    four(c, 1, u(mPT, c), u(mP, c))
                    four(c, 2, u(mP, c), u(mPT, c)).then_inc(pe_l[c], 1)
                for c in range(2):
                    pe.wait_ge(act_l[c], bt * NA + 3)
                    pe.wait_ge(dve_l[c], bt * ND[c] + 8)
                    four(c, 3, u(mA, c), u(mE, c)).then_inc(pe_l[c], 1)
                for c in range(2):
                    pe.wait_ge(act_l[c], bt * NA + 4)
                    four(c, 1, u(mAT, c), u(mA, c)).then_inc(pe_l[c], 1)
                for c in range(2):
                    pe.wait_ge(act_l[c], bt * NA + 5)
                    pe.wait_ge(dve_l[c], bt * ND[c] + 9)
                    four(c, 3, u(mP, c), u(mE, c)).then_inc(pe_l[c], 1)
                for lv in range(3):
                    for c in range(2):
                        pe.wait_ge(dve_l[c], bt * ND[c] + 10 + 2 * lv)
                        for i in range(4):
                            last = nc.tensor.transpose(U4(ps[4 * c], i), U4(mE[:, c, :], i), C("ident"))
                        last.then_inc(pe_l[c], 1)
                    for c in range(2):
                        four(c, 1, u(mL, c), u(mE, c)).then_inc(pe_l[c], 1)
                    for c in range(2):
                        pe.wait_ge(act_l[c], bt * NA + 6 + lv)
                        pe.wait_ge(dve_l[c], bt * ND[c] + 11 + 2 * lv)
                        four(c, 2, u(mPT, c), u(mP, c)).then_inc(pe_l[c], 1)
                for c in range(2):
                    pe.wait_ge(dve_l[c], bt * ND[c] + 16)
                    if c:
                        pe.wait_ge(dve_l[0], bt * ND[0] + 17)
                    for i in range(4):
                        z = Q4(ps[4 * c + 3], i)
                        last = mm(z, U4(mAK[:, c, :], i), vtok[:, c, hcol(i)], start=True, stop=not c)
                        if c:
                            last = mm(z, KK[rows, m0 + i, tok(1)], st[rows, m0 + i, :], start=False, stop=True)
                    last.then_inc(pe_l[c], 1)
                    pe.wait_ge(act_l[c], bt * NA + 9)
                    for i in range(4):
                        last = mm(Q4(ps[4 * c + 1], i), U4(mE[:, c, :], i), Q4(zb[:, c, :], i), start=True, stop=True)
                    last.then_inc(pe_l[c], 1)
                    pe.wait_ge(act_l[c], bt * NA + 10)
                    if not c:
                        for i in range(4):
                            o = ps[3][rows, i * HEAD:(i + 1) * HEAD]
                            mm(o, btok[:, hcol(i)], Q4(ub[:, 0, :], i), start=True, stop=False)
                            last = mm(o, ktok[:, hcol(i)], vtok[:, 0, hcol(i)], start=False, stop=True)
                        last.then_inc(pe_l[c], 1)
                    for i in range(4):
                        o = ps[4 * c + 2][rows, i * P:(i + 1) * P]
                        mm(o, Q4(ub[:, c, :], i), U4(mRB[:, c, :], i), start=True, stop=False)
                        last = mm(o, vtok[:, c, hcol(i)], U4(mRK[:, c, :], i), start=False, stop=not c)
                        if c:
                            last = mm(o, st[rows, m0 + i, :], R[rows, m0 + i, tok(1)], start=False, stop=True)
                    last.then_inc(pe_l[c], 1)

            for c in range(2):
                pe.wait_ge(act_l[c], 4 * NA)
            head_sums(flat(i_SW), (0, 1, 2, 3))
            pe.wait_ge(dve_h, 1)
            head_sums(flat(i_TMP), (4, 5, 6, 7))

            pe.wait_ge(merged, 1)
            for half in range(2):
                s, v = chunk_in(NIN + half)
                pe.wait_ge(s, v)
                for t in range(TT):
                    for k in range(KT):
                        last = mm(ps[2 * t + half][:, :], Y[:, k, t * P:(t + 1) * P], chunk(NIN + half)[:, k, :],
                                  start=k == 0, stop=k == KT - 1)
                last.then_inc(wout_done, 1)
            pe.wait_ge(dve_h, 5)
            for k in range(KT):
                b = 4 + k % 2
                if k >= 2:
                    pe.wait_ge(act_h, 3 + k - 1)
                for t in range(TT):
                    last = nc.tensor.transpose(ps[b][:, t * P:(t + 1) * P], HN[:, t, k * P:(k + 1) * P], C("ident"))
                last.then_inc(pe_h, 1)
            pe.wait_ge(act_h, 3 + KT)
            pe.wait_ge(late_in, 16 * 8)
            for t in range(TT):
                for k in range(KT):
                    last = mm(ps[6][:, t * E:(t + 1) * E], HNT[:, k, t * P:(t + 1) * P], rw[:, k, :],
                              start=k == 0, stop=k == KT - 1)
            last.then_inc(pe_h, 1)
            pe.wait_ge(dve_h, 7)
            mm(ps[7][:, 0:E], C("above"), msk[:, 0, :], start=True, stop=True)
            mm(ps[7][:, E:2 * E], C("ones"), msk[:, 0, :], start=True, stop=False)
            mm(ps[7][:, E:2 * E], C("above"), msk[:, 1, :], start=False, stop=True)
            mm(ps[7][:, 2 * E:3 * E], C("ones"), msk[:, 0, :], start=True, stop=False)
            mm(ps[7][:, 2 * E:3 * E], C("ones"), msk[:, 1, :], start=False, stop=True)
            for t in range(TT):
                last = nc.tensor.transpose(ps[5][0:E, t * P:(t + 1) * P], gw[:, t, :], C("ident"))
            last.then_inc(pe_h, 1)
            pe.wait_ge(dve_h, 8)
            for t in range(TT):
                for half in range(2):
                    mm(ps[2 * t + half][:, :], gwT[:, t * P:(t + 1) * P], b2s[0:E, half * 512:half * 512 + 512],
                       start=True, stop=True)

            pe.wait_ge(rounds_in, 1)
            n_rounds = pe.value_load(rounds[0:1, 0:1], min_val=1, max_val=4)
            pe.sem_inc(w_used, 12)
            with pe.Fori(0, n_rounds) as r:
                with pe.Fori(0, E) as e:
                    it = r * E + e
                    pe.wait_ge(sel_ready, (it + 1) * 4)
                    pe.wait_ge(at_ready, it + 1)
                    for k in range(KT):
                        for t in range(TT):
                            for s in range(3):
                                last = mm(ps[6][:, k * CAP:(k + 1) * CAP], H3[:, t, s, k * P:(k + 1) * P],
                                          sel[:, t, :], start=t + s == 0, stop=t + s == 3)
                    last.then_inc(gathered, 1)
                    pe.wait_ge(y_ready, it + 1)
                    for t in range(TT):
                        last = nc.tensor.transpose(ps[7][:, t * P:(t + 1) * P], gsel[:, t, :], C("ident"))
                    last.then_inc(gate_turned, 1)
                    pe.wait_ge(u_free, it + 1)
                    for part in range(2):
                        for half in range(2):
                            last = mm(ps[4 + part][64 * half:64 * half + 64, :], oh[:, :],
                                      b1s[0:3 * E, part * D + half * 512:part * D + half * 512 + 512],
                                      start=True, stop=False)
                    last.then_inc(b1_used, 1)
                    pe.wait_ge(xe_ready, it + 1)
                    for k in range(8):
                        pe.wait_ge(expert_in[k], (it + 1) * 16)
                        for part in range(2):
                            for half in range(2):
                                last = mm(ps[4 + part][64 * half:64 * half + 64, :], xe[:, k * CAP:(k + 1) * CAP],
                                          ring[:, k, part * D + half * 512:part * D + half * 512 + 512],
                                          start=False, stop=k == 7)
                        last.then_inc(w_used, 1)
                    pe.wait_ge(act_ready, it + 1)
                    for c in range(4):
                        last = nc.tensor.transpose(ps[6][:, c * P:(c + 1) * P], actb[:, c * P:(c + 1) * P], C("ident"))
                    last.then_inc(act_turned, 1)
                    pe.wait_ge(at_ready, it + 2)
                    pe.wait_ge(gt_ready, it + 1)
                    for j in range(4):
                        pe.wait_ge(expert_in[8 + j], (it + 1) * 16)
                        for i in range(2):
                            k = 2 * j + i
                            lhs = actT[:, (k % 4) * P + (k // 4) * CAP:(k % 4) * P + (k // 4) * CAP + CAP]
                            for half in range(2):
                                last = mm(ps[7][64 * half:64 * half + 64, :], lhs,
                                          ring[:, 8 + j, i * D + half * 512:i * D + half * 512 + 512],
                                          start=k == 0, stop=k == 7)
                        last.then_inc(w_used, 1)
                    pe.wait_ge(y_ready, it + 2)
                    for t in range(TT):
                        for half in range(2):
                            last = mm(ps[2 * t + half][:, :], gts[64 * half:64 * half + 64, t * P:(t + 1) * P],
                                      yb[64 * half:64 * half + 64, :], start=False, stop=False, skip_group_check=True)
                    last.then_inc(combined, 1)

        @block.scalar
        def _(act):
            af = nc.scalar.activation
            act.wait_ge(x_in, 16)
            for t in range(TT):
                af(flat(i_SW)[:, 0:D], flat(i_G2)[:, t * D:(t + 1) * D], ACT.Square,
                   accum_out=col[:, t:t + 1]).then_inc(act_rms, 1)
                act.wait_ge(act_rms, t + 1)
            act.wait_ge(dve_rms, 1)
            af(col[:, 4:6], col[:, 2:4], ACT.Sqrt).then_inc(act_rms, 1)
            for k in range(KT):
                act.wait_ge(xt_done, k + 1)
                af(XN[:, k, :], ps[k % 4][:, 0:T], ACT.Copy, scale=pc("norm_mix_g", k)).then_inc(xn_ready, 1)
            act.wait_ge(dve_rms, 3)
            for b in range(N_SHIFT):
                h = blocks[b][2]
                act.wait_ge(blk_done, b + 1)
                af(shifted(b), ps[b % 4][0:h, 0:T], ACT.Copy, scale=inv[0:h, b:b + 1]).then_inc(blk_scaled, 1)
                if b == 2:
                    act.wait_ge(blk_shifted, 3)
                    af(CS[0:64, 0, :], CS[0:64, 0, :], ACT.Tanh).then_inc(lora_act, 1)
                    af(CS[:, 1, :], CS[:, 1, :], ACT.Sigmoid).then_inc(lora_act, 1)
                    af(CS[0:32, 2, :], CS[0:32, 2, :], ACT.Sigmoid).then_inc(lora_act, 1)
            act.wait_ge(dve_rms, 2)
            act.wait_ge(xt_done, KT)
            b = N_SHIFT
            for kind, dst in enumerate((SW, AA, G, GC, XI, GB, G1, G2)):
                for m in range(KT):
                    act.wait_ge(blk_done, b + 1)
                    o, i = dst[:, m, :], ps[b % 4][:, 0:T]
                    if kind == 0:
                        af(o, i, ACT.Sigmoid, bias=pc("w0", m)).then_inc(blk_copied, 1)
                    elif kind == 1:
                        af(o, i, ACT.Sigmoid, bias=pc("a0", m)).then_inc(blk_copied, 1)
                    elif kind < 6:
                        af(o, i, ACT.Copy).then_inc(blk_copied, 1)
                    else:
                        af(o, i, ACT.Sigmoid).then_inc(blk_copied, 1)
                    b += 1
                if kind == 3:
                    act.wait_ge(dve_step, 2)
                    af(flat(i_TMP), flat(i_TMP), ACT.Sqrt).then_inc(act_step, 1)
                if kind == 4:
                    act.wait_ge(dve_step, 3)
                    af(flat(i_SW), flat(i_SW), ACT.Exp, scale=-KAPPA).then_inc(act_step, 1)
                    af(flat(i_TMP), flat(i_CS), ACT.Exp, scale=-KAPPA).then_inc(act_step, 1)
                    act.wait_ge(act_step, 3)
                    af(flat(i_CS), flat(i_CS), ACT.Exp, scale=KAPPA).then_inc(act_step, 1)
                    af(dec[:], dec[:], ACT.Exp, scale=-KAPPA).then_inc(act_step, 1)
            for n in range(8):
                dst = (vtok[:, 0], vtok[:, 1], btok[:], ktok[:])[n // 2][:, 512 * (n % 2):512 * (n % 2) + 512]
                act.wait_ge(pe_tok, n + 1)
                af(dst, ps[n][:, :], ACT.Copy).then_inc(act_tok, 1)
            act.wait_ge(dve_step, 6)
            for bt in range(4):
                q, m0 = bt // 2, 4 * (bt % 2)
                rows = slice(64 * q, 64 * q + 64)
                n_pe = lambda c, k: bt * NPE[c] + k

                def take(c, k, dst, bank):
                    act.wait_ge(pe_l[c], n_pe(c, k))
                    af(dst[:, c, :], ps[4 * c + bank][:, :], ACT.Copy).then_inc(act_l[c], 1)

                for k, first, second in ((4, mP, mPT), (6, mA, mAT)):
                    for c in range(2):
                        take(c, k, first, 1)
                        take(c, k, second, 2)
                for c in range(2):
                    act.wait_ge(pe_l[c], n_pe(c, 7))
                    take(c, 8, mP, 1)
                for lv in range(3):
                    for c in range(2):
                        take(c, 10 + 3 * lv, mPT, 0)
                for c in range(2):
                    act.wait_ge(pe_l[c], n_pe(c, 19))
                    af(zb[:, c, :], ps[4 * c + 3][:, 0:4 * HEAD], ACT.Copy).then_inc(act_l[c], 1)
                    act.wait_ge(pe_l[c], n_pe(c, 20))
                    af(ub[:, c, :], ps[4 * c + 1][:, 0:4 * HEAD], ACT.Copy).then_inc(act_l[c], 1)
                    act.wait_ge(pe_l[c], n_pe(c, NPE[c]))
                    af(Y[rows, m0:m0 + 4, c * P:(c + 1) * P],
                       ps[4 * c + 2][rows, :].rearrange("p (m t) -> p m t", m=4), ACT.Copy).then_inc(act_l[c], 1)
            act.wait_ge(dve_h, 2)
            af(flat(i_TMP), flat(i_TMP), ACT.Sqrt).then_inc(act_h, 1)
            act.wait_ge(dve_h, 3)
            for t in range(TT):
                af(HN[:, t, :], HB[:, t, :], ACT.Square, accum_out=col[:, 8 + t:9 + t]).then_inc(act_chain, 1)
            act.wait_ge(act_chain, TT)
            act.sem_inc(act_h, 1)
            act.wait_ge(dve_h, 4)
            af(col[:, 12:14], col[:, 10:12], ACT.Sqrt).then_inc(act_h, 1)
            for k in range(KT):
                act.wait_ge(pe_h, k + 1)
                af(HNT[:, k, :], ps[4 + k % 2][:, 0:T], ACT.Copy).then_inc(act_h, 1)
            act.wait_ge(dve_h, 6)
            af(ge[:, :, 0:TOP], ge[:, :, 0:TOP], ACT.Exp).then_inc(act_h, 1)

            act.wait_ge(rounds_in, 1)
            n_rounds = act.value_load(rounds[0:1, 0:1], min_val=1, max_val=4)
            act.sem_inc(at_ready, 1)
            with act.Fori(0, n_rounds) as r:
                with act.Fori(0, E) as e:
                    it = r * E + e
                    act.wait_ge(gathered, it + 1)
                    act.wait_ge(w_used, it * 12 + 8)
                    af(xe, ps[6][:, :], ACT.Copy).then_inc(xe_ready, 1)
                    act.wait_ge(glu_ready, it + 1)
                    af(sig, glu, ACT.Sigmoid, scale=ALPHA).then_inc(sig_ready, 1)
                    act.wait_ge(act_turned, it + 1)
                    af(actT, ps[6][:, :], ACT.Copy).then_inc(at_ready, 1)
            act.wait_ge(dve_h, 9)
            for t in range(TT):
                af(HN[:, t, :], HB[:, t, :], ACT.Square, accum_out=col[:, 16 + t:17 + t]).then_inc(act_chain, 1)
            act.wait_ge(act_chain, 2 * TT)
            act.sem_inc(act_h, 1)
            act.wait_ge(dve_h, 10)
            af(col[:, 20:22], col[:, 18:20], ACT.Sqrt).then_inc(act_h, 1)

        @block.vector
        def _(v):
            tt, ts, stt, cp = nc.vector.tensor_tensor, nc.vector.tensor_scalar, nc.vector.scalar_tensor_tensor, nc.vector.tensor_copy
            linked = [0]

            def link(ins):
                linked[0] += 1
                ins.then_inc(dve_chain, 1)
                v.wait_ge(dve_chain, linked[0])

            def per_feature(name, n=T):
                return par[:, P_AT[name]:P_AT[name] + KT].unsqueeze(2).to_broadcast([P, KT, n])

            def root_mean(src, dst, signal):
                ts(col[:, dst:dst + 2], col[:, src:src + 2], 1.0 / D, NORM_EPS, ALU.mult, ALU.add).then_inc(signal, 1)

            v.wait_ge(act_rms, 2)
            root_mean(0, 2, dve_rms)
            v.wait_ge(act_rms, 3)
            link(nc.vector.reciprocal(col[:, 6:8], col[:, 4:6]))
            for t in range(TT):
                last = ts(ring[:, 11, t * D:(t + 1) * D], flat(i_G2)[:, t * D:(t + 1) * D], col[:, 6 + t:7 + t], None, ALU.mult)
                last.then_inc(xt_ready, 1)
            v.wait_ge(xt_ready, 2)
            v.sem_inc(dve_rms, 1)
            v.wait_ge(const_in, 32)
            link(ts(inv[:, 0:3], par[:, P_AT["mu_lora"]:P_AT["mu_lora"] + 3], -1.0, 1.0, ALU.mult, ALU.add))
            for i, n in enumerate(("mu_k", "mu_r", "mu_v", "k_a")):
                link(ts(inv[:, 3 + 8 * i:11 + 8 * i], par[:, P_AT[n]:P_AT[n] + 8], -1.0, 1.0, ALU.mult, ALU.add))
            v.sem_inc(dve_rms, 1)
            for b in range(N_SHIFT):
                h = blocks[b][2]
                mu = pc("mu_lora", b, h) if b < 3 else pc(("mu_k", "mu_r", "mu_v")[(b - 3) // 8], (b - 3) % 8)
                v.wait_ge(blk_scaled, b + 1)
                o = shifted(b)
                stt(o[:, 1:T], ps[b % 4][0:h, 0:T - 1], mu, o[:, 1:T], ALU.mult, ALU.add).then_inc(blk_shifted, 1)
            v.wait_ge(blk_shifted, N_SHIFT)
            link(tt(KK, Kt, per_feature("k_k"), ALU.mult))
            tt(TMP, KK, KK, ALU.mult).then_inc(dve_step, 1)
            v.wait_ge(blk_copied, 3 * KT)
            link(nc.vector.memset(flat(i_BON), 1.0))
            link(nc.vector.memset(flat(i_BON).rearrange("p (c t) -> p c t", t=P)[:, :, 0:1], 0.0))
            link(nc.vector.tensor_tensor_scan(flat(i_CS), flat(i_BON), flat(i_SW), 0.0, ALU.mult, ALU.add))
            cs4 = flat(i_CS).rearrange("p (m c t) -> p m c t", m=KT, c=TT)
            link(cp(cm[:], cs4[:, :, :, HEAD - 1]))
            link(cp(ce[:], cs4[:, :, :, P - 1]))
            link(tt(dec[:], ce[:, :, 0], cm[:, :, 0], ALU.subtract))
            link(tt(dec[:], dec[:], cm[:, :, 1], ALU.add))
            cs3 = flat(i_CS).rearrange("p (c t) -> p c t", t=P)
            link(tt(cs3, cs3, cm[:].rearrange("p m c -> p (m c)").unsqueeze(2).to_broadcast([P, 2 * KT, P]), ALU.subtract))
            link(tt(SW, CS, SW, ALU.subtract))
            v.wait_ge(pe_sum, 1)
            for i in range(4):
                last = ts(flat(i_TMP)[:, 512 * i:512 * i + 512], ps[4 + i][:, :], 1e-24, None, ALU.max)
            link(last)
            v.sem_inc(dve_step, 1)
            v.wait_ge(act_step, 1)
            link(nc.vector.reciprocal(flat(i_TMP), flat(i_TMP)))
            link(tt(KK, KK, TMP, ALU.mult))
            v.sem_inc(dve_step, 1)
            link(tt(BON, AA, per_feature("k_a"), ALU.mult))
            link(tt(BON, BON, inv[:, 27:35].unsqueeze(2).to_broadcast([P, KT, T]), ALU.add))
            link(tt(Kt, Kt, BON, ALU.mult))
            link(tt(AA, KK, AA, ALU.mult))
            link(tt(BON, R, Kt, ALU.mult))
            link(tt(BON, BON, per_feature("r_k"), ALU.mult))
            v.sem_inc(dve_step, 1)
            v.wait_ge(act_step, 5)
            link(stt(flat_ring(7), flat_ring(7), -1.0, flat(i_SW), ALU.mult, ALU.mult))
            link(tt(R, R, TMP, ALU.mult))
            link(tt(AA, AA, CS, ALU.mult))
            link(tt(Kt, Kt, CS, ALU.mult))
            v.wait_ge(pe_sum, 2)
            for i in range(4):
                s_ = slice(512 * i, 512 * i + 512)
                last = tt(flat(i_BON)[:, s_], ps[4 + i][:, :], flat_ring(10)[:, s_], ALU.mult)
            link(last)
            v.sem_inc(dve_step, 1)
            v.wait_ge(blk_copied, 8 * KT)
            link(tt(GC, GC, XI, ALU.mult))
            link(tt(XI, GC, per_feature("conv2"), ALU.mult))
            for back, name in ((1, "conv1"), (2, "conv0")):
                for m in range(KT):
                    last = stt(XI[:, m, back:], GC[:, m, 0:T - back], pc(name, m), XI[:, m, back:], ALU.mult, ALU.add)
                link(last)
            link(tt(XI, XI, GB, ALU.mult))
            link(tt(XI, XI, G1, ALU.mult))
            v.sem_inc(dve_step, 1)

            b4 = lambda t: t.rearrange("p (i n) -> p i n", i=4)
            mask = lambda n: C(n).unsqueeze(1).to_broadcast([P, 4, P])
            for bt in range(4):
                q, m0 = bt // 2, 4 * (bt % 2)
                rows = slice(64 * q, 64 * q + 64)

                def at(c, k):
                    v.wait_ge(pe_l[c], bt * NPE[c] + k)

                def done(c, ins):
                    ins.then_inc(dve_l[c], 1)

                def own(c, k):
                    v.wait_ge(dve_l[c], bt * ND[c] + k)

                for c in range(2):
                    at(c, 1)
                    done(c, tt(b4(mAT[:, c, :]), b4(ps[4 * c][:, :]), mask("above16"), ALU.mult))
                    done(c, tt(b4(mA[:, c, :]), b4(ps[4 * c + 1][:, :]), mask("below16"), ALU.mult))
                    done(c, tt(b4(mL[:, c, :]), b4(ps[4 * c + 1][:, :]), mask("below"), ALU.mult))
                    own(c, 1)
                    done(c, tt(b4(mE[:, c, :]), b4(mAT[:, c, :]), mask("ident"), ALU.add))
                for c in range(2):
                    at(c, 2)
                    done(c, tt(b4(mAK[:, c, :]), b4(ps[4 * c + 2][:, :]), mask("above"), ALU.mult))
                    done(c, tt(b4(mRK[:, c, :]), b4(ps[4 * c + 3][:, :]), mask("above_eq"), ALU.mult))
                for c in range(2):
                    at(c, 3)
                    done(c, tt(b4(mRB[:, c, :]), b4(ps[4 * c][:, :]), mask("above_eq"), ALU.mult))
                for k, n in ((5, 4), (7, 8), (9, 9)):
                    for c in range(2):
                        at(c, k)
                        own(c, n)
                        done(c, tt(mE[:, c, :], mE[:, c, :], ps[4 * c + 3][:, :], ALU.add))
                for lv in range(3):
                    for c in range(2):
                        at(c, 11 + 3 * lv)
                        done(c, tt(b4(mP[:, c, :]), b4(ps[4 * c + 1][:, :]), mask(("pair16", "pair32", "pair64")[lv]), ALU.mult))
                    for c in range(2):
                        at(c, 12 + 3 * lv)
                        own(c, 10 + 2 * lv)
                        done(c, tt(mE[:, c, :], mE[:, c, :], ps[4 * c + 2][:, :], ALU.add))
                at(0, 21)
                done(0, tt(st[rows, m0:m0 + 4, :], ps[3][rows, 0:4 * HEAD].rearrange("p (m n) -> p m n", m=4),
                           dec[rows, m0:m0 + 4].unsqueeze(2).to_broadcast([64, 4, HEAD]), ALU.mult))
            v.wait_ge(pe_sum, 3)
            for i in range(4):
                s_ = slice(512 * i, 512 * i + 512)
                last = stt(flat(i_SW)[:, s_], ps[i][:, :], -1.0 / HEAD, flat(i_SW)[:, s_], ALU.mult, ALU.add)
            link(last)
            link(tt(TMP, Y, Y, ALU.mult))
            v.sem_inc(dve_h, 1)
            v.wait_ge(pe_sum, 4)
            for i in range(4):
                last = ts(flat(i_TMP)[:, 512 * i:512 * i + 512], ps[4 + i][:, :], 1.0 / HEAD, GN_EPS, ALU.mult, ALU.add)
            link(last)
            v.sem_inc(dve_h, 1)
            v.wait_ge(act_h, 1)
            link(nc.vector.reciprocal(flat(i_TMP), flat(i_TMP)))
            link(tt(Y, Y, TMP, ALU.mult))
            link(tt(Y, Y, per_feature("ln_g"), ALU.mult))
            link(tt(Y, Y, per_feature("ln_b"), ALU.add))
            link(tt(Y, Y, BON, ALU.add))
            link(tt(Y, Y, G, ALU.mult))
            link(tt(Y, Y, G2, ALU.mult))
            link(tt(Y, Y, XI, ALU.add))
            v.sem_inc(merged, 1)
            v.wait_ge(wout_done, 2)
            v.wait_ge(xres_in, 16)
            for t in range(TT):
                for half in range(2):
                    s_ = slice(512 * half, 512 * half + 512)
                    last = tt(HB[:, t, s_], HB[:, t, s_], ps[2 * t + half][:, :], ALU.add)
            link(last)
            v.sem_inc(dve_h, 1)
            v.wait_ge(act_h, 2)
            root_mean(8, 10, dve_h)
            v.wait_ge(act_h, 3)
            link(nc.vector.reciprocal(col[:, 14:16], col[:, 12:14]))
            v.wait_ge(late_in, 16 * 8)
            for t in range(TT):
                last = stt(HN[:, t, :], HB[:, t, :], col[:, 14 + t:15 + t], gffn, ALU.mult, ALU.mult)
            link(last)
            v.sem_inc(dve_h, 1)
            for t in range(TT):
                link(cp(H3[:, t, 0, :], HN[:, t, :]))
                link(tt(h3tmp, HN[:, t, :], H3[:, t, 0, :], ALU.subtract))
                link(cp(H3[:, t, 1, :], h3tmp))
                link(tt(h3tmp, h3tmp, H3[:, t, 1, :], ALU.subtract))
                link(cp(H3[:, t, 2, :], h3tmp))
            nb = 3 * E
            link(cp(b1s[0:nb, :], b1f[0:nb, :]))
            link(tt(b1f[0:nb, :], b1f[0:nb, :], b1s[0:nb, :], ALU.subtract))
            link(cp(b1m[:], b1f[0:nb, :]))
            link(cp(b1s[E:2 * E, :], b1m[E:2 * E, :]))
            link(tt(b1f[2 * E:nb, :], b1f[2 * E:nb, :], b1m[2 * E:nb, :], ALU.subtract))
            link(cp(b1s[2 * E:nb, :], b1f[2 * E:nb, :]))
            v.wait_ge(pe_h, 9)
            link(tt(lg, ps[6][:, 0:TT * E].rearrange("p (t e) -> p t e", t=TT),
                    rb.unsqueeze(1).to_broadcast([P, TT, E]), ALU.add))
            for t in range(TT):
                link(nc.vector.max(mx[:, t, :], lg[:, t, :]))
                link(nc.vector.max_index(mi[:, t, :], mx[:, t, :], lg[:, t, :]))
            link(cp(mif[:], mi[:]))
            link(tt(ge[:, :, 0:TOP], mx[:, :, 0:TOP], mx[:, :, 0:1].to_broadcast([P, TT, TOP]), ALU.subtract))
            v.sem_inc(dve_h, 1)
            v.wait_ge(act_h, 4 + KT)
            link(nc.vector.tensor_reduce(cnt[:, 0:TT], ge[:, :, 0:TOP], AX_X, ALU.add))
            link(nc.vector.reciprocal(cnt[:, 2:2 + TT], cnt[:, 0:TT]))
            link(tt(ge[:, :, 0:TOP], ge[:, :, 0:TOP], cnt[:, 2:2 + TT].unsqueeze(2).to_broadcast([P, TT, TOP]), ALU.mult))
            for t in range(TT):
                for k in range(TOP):
                    one, idx = (gw, msk)[0][:, t, :], mif[:, t, k:k + 1]
                    if k == 0:
                        ts(one, C("expert", E), idx, ge[:, t, k:k + 1], ALU.is_equal, ALU.mult)
                        link(ts(msk[:, t, :], C("expert", E), idx, None, ALU.is_equal))
                    else:
                        link(ts(lg[:, t, :], C("expert", E), idx, ge[:, t, k:k + 1], ALU.is_equal, ALU.mult))
                        link(tt(one, one, lg[:, t, :], ALU.add))
                        link(stt(msk[:, t, :], C("expert", E), idx, msk[:, t, :], ALU.is_equal, ALU.add))
            v.sem_inc(dve_h, 1)
            v.wait_ge(pe_h, 10)
            link(ts(rk[:], msk[:], -FAR, FAR, ALU.mult, ALU.add))
            link(tt(rk[:], rk[:], ps[7][:, 0:2 * E].rearrange("p (t e) -> p t e", t=TT), ALU.add))
            link(cp(gwT, ps[5][0:E, 0:T]))
            v.sem_inc(dve_h, 1)
            link(nc.vector.tensor_reduce(cnt[:, 4:5], ps[7][:, 2 * E:3 * E], AX_X, ALU.max))
            link(ts(cnt[:, 5:6], cnt[:, 4:5], float(CAP), 1.0, ALU.is_gt, ALU.add))
            for n in range(2, T // CAP):
                link(stt(cnt[:, 5:6], cnt[:, 4:5], float(n * CAP), cnt[:, 5:6], ALU.is_gt, ALU.add))
            link(cp(rounds[:], cnt[:, 5:6]))
            v.sem_inc(rounds_in, 1)
            n_rounds = v.value_load(rounds[0:1, 0:1], min_val=1, max_val=4)
            v.sem_inc(u_free, 1)
            v.sem_inc(y_ready, 1)
            with v.Fori(0, n_rounds) as r:
                with v.Fori(0, E) as e:
                    it = r * E + e
                    tt(sel[:], C("slot", CAP).unsqueeze(1).to_broadcast([P, TT, CAP]),
                       rk[:, :, bass.ds(e, 1)].to_broadcast([P, TT, CAP]), ALU.is_equal).then_inc(sel_ready, 1)
                    for t in range(TT):
                        ts(gsel[:, t, :], C("slot"), rk[:, t, bass.ds(e, 1)], gw[:, t, bass.ds(e, 1)],
                           ALU.is_equal, ALU.mult).then_inc(sel_ready, 1)
                    ts(oh[:], C("ones", CAP)[0:3 * E], cst[0:3 * E, bass.ds(e + C_AT["pick"], 1)], None,
                       ALU.mult).then_inc(sel_ready, 1)
                    v.wait_ge(gate_turned, it + 1)
                    cp(gts[:, 0:T], ps[7][:, 0:T]).then_inc(gt_ready, 1)
                    v.wait_ge(w_used, it * 12 + 20)
                    ts(glu, ps[4][:, :], LIMIT, None, ALU.min).then_inc(glu_ready, 1)
                    ts(lin, ps[5][:, :], LIMIT, -LIMIT, ALU.min, ALU.max).then_inc(u_free, 1)
                    v.wait_ge(u_free, it + 2)
                    v.wait_ge(glu_ready, it + 1)
                    stt(lin, lin, 1.0, glu, ALU.add, ALU.mult).then_inc(lin_ready, 1)
                    v.wait_ge(sig_ready, it + 1)
                    v.wait_ge(lin_ready, it + 1)
                    tt(actb, lin, sig, ALU.mult).then_inc(act_ready, 1)
                    v.wait_ge(w_used, it * 12 + 24)
                    cp(yb, ps[7][:, :]).then_inc(y_ready, 1)
                ts(rk[:], rk[:], -float(CAP), None, ALU.add).then_inc(round_ready, 1)
                v.wait_ge(round_ready, r + 1)
            v.wait_ge(combined, n_rounds * E)
            for t in range(TT):
                for half in range(2):
                    s_ = slice(512 * half, 512 * half + 512)
                    last = tt(HB[:, t, s_], HB[:, t, s_], ps[2 * t + half][:, :], ALU.add)
            link(last)
            v.sem_inc(dve_h, 1)
            v.wait_ge(act_h, 5 + KT)
            root_mean(16, 18, dve_h)
            v.wait_ge(act_h, 6 + KT)
            link(nc.vector.reciprocal(col[:, 22:24], col[:, 20:22]))
            for t in range(TT):
                last = stt(HB[:, t, :], HB[:, t, :], col[:, 22 + t:23 + t], gfin, ALU.mult, ALU.mult)
            link(last)
            v.sem_inc(out_ready, 1)


_DIRECT = ["x", "w_in", "w_out", "norm_ffn_g", "norm_final_g", "decay_w2", "iclr_a2", "gate_g2", "router_w",
           "router_b", "exp_w1", "exp_b1", "exp_w2", "exp_b2"]


def kernel(**inputs):
    import concourse.bacc as bacc
    from concourse.bass_utils import run_bass_kernel_spmd

    nc = bacc.Bacc("TRN2", target_bir_lowering=False, num_devices=1)
    arrays = {n: np.ascontiguousarray(inputs[n]) for n in _DIRECT}
    mu = np.asarray(inputs["shift_mu"])[0]
    lora = np.concatenate([mu[3 * D:], np.zeros(3 * P - LORA, np.float32)])
    conv = np.asarray(inputs["conv_w"])[0]
    one = lambda n: np.asarray(inputs[n]).reshape(-1)
    parts = [one("norm_mix_g"), mu[0:D], mu[D:2 * D], mu[2 * D:3 * D], lora, one("decay_w0"), one("iclr_a0"),
             one("k_k"), one("k_a"), one("r_k"), one("ln_x_g"), one("ln_x_b"), conv[0], conv[1], conv[2]]
    arrays["params"] = np.ascontiguousarray(np.concatenate([p.reshape(-1, P) for p in parts]).T)
    arrays["consts"] = constants()
    args = [nc.dram_tensor(f"in_{n}", a.shape, mybir.dt.from_np(a.dtype), kind="ExternalInput").ap()
            for n, a in arrays.items()]
    args.append(nc.dram_tensor("out_0", (1, T, D), F32, kind="ExternalOutput").ap())
    build(nc, *args)
    r = run_bass_kernel_spmd(nc, [{f"in_{n}": a for n, a in arrays.items()}], core_ids=[0])
    return r.results[0]["out_0"]
```

```python
from contextlib import ExitStack

import numpy as np

import concourse.bass as bass
from concourse import mybir

ALU = mybir.AluOpType
ACT = mybir.ActivationFunctionType
F32 = mybir.dt.float32
BF16 = mybir.dt.bfloat16
I32 = mybir.dt.int32
U32 = mybir.dt.uint32
AX_X = mybir.AxisListType.X

P = 128
T = 256
D = 1024
TT = T // P
KT = D // P
HEAD = 64
E = 32
TOP = 4
CAP = 64
NORM_EPS, GN_EPS = 1e-5, 64e-5
ALPHA, LIMIT = 1.702, 7.0
KAPPA = float(np.exp(-0.5))
FAR = 1.0e4

COL_GB, COL_GC, COL_XIN = 0, D, 2 * D
COL_R, COL_K, COL_V = 3 * D, 4 * D, 5 * D
COL_LORA = 6 * D
LORA = 288
COL_GATE_CONV = COL_LORA + LORA
COL_GATE_RWKV = COL_GATE_CONV + D
CHUNK = 512

CONSTS = ["ident", "above", "above_eq", "below", "below16", "above16", "pair16", "pair32",
          "head_ones", "ones", "slot", "expert", "pick"]
C_AT = {n: i * P for i, n in enumerate(CONSTS)}

PARAMS = [("norm_mix_g", 8), ("mu_r", 8), ("mu_k", 8), ("mu_v", 8), ("mu_lora", 3), ("w0", 8), ("a0", 8),
          ("k_k", 8), ("k_a", 8), ("r_k", 8), ("ln_g", 8), ("ln_b", 8), ("conv0", 8), ("conv1", 8), ("conv2", 8)]
P_AT, _n = {}, 0
for _name, _w in PARAMS:
    P_AT[_name] = _n
    _n += _w
NPAR = _n


def constants():
    p, f = np.arange(P)[:, None], np.arange(P)[None, :]
    pair = lambda b: (p // (2 * b) == f // (2 * b)) & (p // b % 2 == 0) & (f // b % 2 == 1)
    same16 = p // 16 == f // 16
    m = {
        "ident": p == f, "above": f > p, "above_eq": f >= p, "below": f < p,
        "below16": (f < p) & same16, "above16": (f > p) & same16,
        "pair16": pair(16), "pair32": pair(32),
        "head_ones": p // HEAD == f // HEAD, "ones": p == p + 0 * f,
        "slot": f % CAP + 0 * p, "expert": f % E + 0 * p, "pick": (p % E == f % E) & (p < 3 * E),
    }
    return np.concatenate([np.asarray(m[n], np.float32) for n in CONSTS], axis=1)


def build(nc, x, w_in, w_out, norm_ffn_g, norm_final_g, w2, a2, g2, router_w, router_b,
          exp_w1, exp_b1, exp_w2, exp_b2, params, consts, out):
    with ExitStack() as ctx:
        def sb(name, shape, dt=F32):
            return ctx.enter_context(nc.sbuf_tensor(name, shape, dt))

        def sem(name):
            return ctx.enter_context(nc.semaphore(name))

        ring = sb("ring", [P, 12, 2048])
        work = sb("work", [P, 10, 2048])
        arr = lambda t: t.rearrange("p (m t) -> p m t", m=KT)
        Kt, KK, AA, R, V, G1 = (arr(ring[:, 6 + i]) for i in range(6))
        XN, CS, TMP, GC, GB, SW, XI, BON, G, G2 = (arr(work[:, i]) for i in range(10))
        flat = lambda i: work[:, i]
        i_XN, i_CS, i_TMP, i_GC, i_GB, i_SW, i_XI, i_BON, i_G, i_G2 = range(10)
        Y = SW
        cst = sb("cst", [P, len(CONSTS) * P])
        par = sb("par", [P, NPAR])
        inv = sb("inv", [P, 35])
        col = sb("col", [P, 64])
        vtok = sb("vtok", [P, TT, D])
        btok = sb("btok", [P, D])
        ktok = sb("ktok", [P, D])
        zb = sb("zb", [P, 2, 4 * HEAD])
        ub = sb("ub", [P, 2, 4 * HEAD])
        st = sb("st", [P, KT, HEAD])
        cm = sb("cm", [P, KT, 2])
        ce = sb("ce", [P, KT, 2])
        dec = sb("dec", [P, KT])
        C = lambda n, w=P: cst[:, C_AT[n]:C_AT[n] + w]
        pc = lambda n, m, h=P: par[0:h, P_AT[n] + m:P_AT[n] + m + 1]
        ps = [ctx.enter_context(nc.psum_tensor(f"ps{i}", [P, 512], F32)) for i in range(8)]

        ubuf = lambda i, half: flat(i)[:, 1024 * half:1024 * half + 1024].rearrange("p (l n) -> p l n", l=2)
        mL, mA, mAT, mAK = ubuf(i_XN, 0), ubuf(i_XN, 1), ubuf(i_CS, 0), ubuf(i_CS, 1)
        mRK, mRB, mP, mPT = ubuf(i_TMP, 0), ubuf(i_TMP, 1), ubuf(i_GC, 0), ubuf(i_GC, 1)
        mE = ubuf(i_GB, 0)

        const_in = sem("const_in")
        x_in = [sem(f"x_in{t}") for t in range(TT)]
        b1_in = sem("b1_in")
        factors_ready = sem("factors_ready")
        y_centred = sem("y_centred")
        y_var = sem("y_var")
        y_root = sem("y_root")
        lora_in = sem("lora_in")
        slot_in = [sem(f"slot_in{i}") for i in range(12)]
        xres_in = sem("xres_in")
        late_in = sem("late_in")
        gffn_in = sem("gffn_in")
        h3_cast = sem("h3_cast")
        h3_left = sem("h3_left")
        expert_in = [sem(f"expert_in{i}") for i in range(12)]
        merged = sem("merged")
        dve_chain = sem("dve_chain")
        act_chain = sem("act_chain")
        act_rms = sem("act_rms")
        dve_rms = sem("dve_rms")
        xt_ready = sem("xt_ready")
        xn_ready = sem("xn_ready")
        blk_done = sem("blk_done")
        blk_scaled = sem("blk_scaled")
        blk_shifted = sem("blk_shifted")
        blk_copied = sem("blk_copied")
        lora_act = sem("lora_act")
        dve_step = sem("dve_step")
        pe_sum = sem("pe_sum")
        act_step = sem("act_step")
        pe_tok = sem("pe_tok")
        act_tok = sem("act_tok")
        pe_l = [sem(f"pe_l{i}") for i in range(2)]
        dve_l = [sem(f"dve_l{i}") for i in range(2)]
        act_l = [sem(f"act_l{i}") for i in range(2)]
        z_done = [sem(f"z_done{i}") for i in range(2)]
        z_taken = [sem(f"z_taken{i}") for i in range(2)]
        u_made = [sem(f"u_made{i}") for i in range(2)]
        u_taken = [sem(f"u_taken{i}") for i in range(2)]
        y_made = [sem(f"y_made{i}") for i in range(2)]
        y_taken = [sem(f"y_taken{i}") for i in range(2)]
        s_made = sem("s_made")
        s_taken = sem("s_taken")
        wout_done = sem("wout_done")
        xt_done = sem("xt_done")
        dve_h = sem("dve_h")
        act_h = sem("act_h")
        pe_h = sem("pe_h")
        rounds_in = sem("rounds_in")
        gates_copied = sem("gates_copied")
        sel_ready = sem("sel_ready")
        gathered = sem("gathered")
        gate_turned = sem("gate_turned")
        xe_ready = sem("xe_ready")
        gt_ready = sem("gt_ready")
        b1_used = sem("b1_used")
        w_used = sem("w_used")
        u_free = sem("u_free")
        glu_ready = sem("glu_ready")
        sig_ready = sem("sig_ready")
        act_ready = sem("act_ready")
        act_turned = sem("act_turned")
        at_ready = sem("at_ready")
        y_ready = sem("y_ready")
        combined = sem("combined")
        out_ready = sem("out_ready")
        out_done = sem("out_done")
        lin_ready = sem("lin_ready")
        round_ready = sem("round_ready")

        stream = [(w_in, COL_LORA, LORA)]
        for c0 in (COL_K, COL_R, COL_V, COL_GC, COL_XIN, COL_GB, COL_GATE_CONV, COL_GATE_RWKV):
            stream += [(w_in, c0, CHUNK), (w_in, c0 + CHUNK, CHUNK)]
        NIN = len(stream)
        stream += [(w_out, 0, CHUNK), (w_out, CHUNK, CHUNK)]

        def chunk(n):
            s = 2 * (n % 3)
            return ring[:, s:s + 2, :].rearrange("p s c -> p (s c)").rearrange("p (k c) -> p k c", k=KT)

        def chunk_in(n):
            return slot_in[2 * (n % 3)], 16 * (n // 3 + 1)

        blocks = [(0, 0, P), (0, P, P), (0, 2 * P, 32)]
        for n in range(1, NIN):
            blocks += [(n, i * P, P) for i in range(CHUNK // P)]
        N_SHIFT = 27

        def blocks_until(n):
            last = max(i for i, blk in enumerate(blocks) if blk[0] == n)
            return last + 1 + (3 * KT if last >= N_SHIFT else 0)

        NPE, ND, NA = 18, 16, 8

        def flat_ring(i):
            return ring[:, i]

        def shifted(b):
            n, _, h = blocks[b]
            if b < 3:
                return CS[0:h, b, :]
            return (Kt, R, V)[(b - 3) // 8][:, (b - 3) % 8, :]

        SLOT = [2, 3, 11, 6, 7, 8, 9, 10, 0, 1, 4, 5]

        HB = flat(i_XN).rearrange("p (t d) -> p t d", t=TT)
        HN = flat(i_CS).rearrange("p (t d) -> p t d", t=TT)
        HNT = arr(flat(i_TMP))
        H3 = work[:, i_GC:i_GC + 2].rearrange("p a n -> p (a n)")[:, 0:3072].bitcast(BF16).rearrange(
            "p (t s d) -> p t s d", t=TT, s=3)
        h3tmp = (flat(i_GB)[:, 1024:2048], btok[:])
        b1f = flat(i_XI)
        b1s = flat(i_G2)[:, 0:1024].bitcast(BF16)
        b1m = flat(i_G2)[0:3 * E, 1024:2048].bitcast(BF16)
        gffn = flat(i_G)[:, 0:1024]
        gfin = flat(i_G)[:, 1024:2048]
        b2s = flat(i_BON)[:, 0:1024]
        yt = flat(i_GB)[:, 1024:2048]
        xe, glu, sig, lin = (flat(i_XI)[:, 512 * i:512 * i + 512] for i in range(4))
        actb, actT, yb, gts = (flat(i_SW)[:, 512 * i:512 * i + 512] for i in range(4))
        late = vtok[:].rearrange("p c d -> p (c d)")
        rw = late[:, 0:KT * E].rearrange("p (k e) -> p k e", k=KT)
        rb = late[:, 256:256 + E]
        lg = late[:, 320:320 + TT * E].rearrange("p (t e) -> p t e", t=TT)
        mx = sb("mx", [P, TT, 8])
        mi = sb("mi", [P, TT, 8], U32)
        mif = sb("mif", [P, TT, 8])
        ge = sb("ge", [P, TT, 8])
        gw = sb("gw", [P, TT, E + 1])
        msk = sb("msk", [P, TT, E])
        rk = sb("rk", [P, TT, E + 1])
        hot = ktok[:, 512:512 + TT * TOP * E].rearrange("p (t e k) -> p t e k", t=TT, k=TOP)
        gwT = late[0:E, 512:512 + T]
        cnt = sb("cnt", [P, 8])
        rounds = sb("rounds", [P, 1], I32)
        sel = sb("sel", [P, TT, CAP], BF16)
        gsel = ktok[:, 0:T].rearrange("p (t n) -> p t n", t=TT)
        oh = sb("oh", [3 * E, CAP], BF16)

        block = ctx.enter_context(nc.Block())

        @block.sync
        def _(sp):
            for t in range(TT):
                sp.dma_start(flat(i_G2)[:, t * D:(t + 1) * D], x[0, t * P:(t + 1) * P, :]).then_inc(x_in[t], 16)
            sp.dma_start(cst[:], consts).then_inc(const_in, 16)
            sp.dma_start(par[:], params).then_inc(const_in, 16)
            for n, (w, c0, width) in enumerate(stream):
                if n >= 3:
                    sp.wait_ge(blk_done, blocks_until(n - 3))
                s, _ = chunk_in(n)
                sp.dma_start(chunk(n)[:, :, 0:width],
                             w[0].rearrange("(k p) n -> p k n", p=P)[:, :, c0:c0 + width]).then_inc(s, 16)
                if n == 2:
                    sp.dma_start(flat(i_GB)[0:64, 0:D], w2[0]).then_inc(lora_in, 16)
                    sp.dma_start(flat(i_GB)[64:128, 0:D], a2[0]).then_inc(lora_in, 16)
                    sp.dma_start(flat(i_GB)[:, D:2 * D], g2[0, 0:P]).then_inc(lora_in, 16)
                    sp.dma_start(flat(i_XI)[0:32, 0:D], g2[0, P:P + 32]).then_inc(lora_in, 16)

            def load_expert(e, it):
                for j in range(12):
                    sp.wait_ge(w_used, it * 12 + j + 1)
                    if j < 8:
                        src = exp_w1[0, bass.ds(e, 1), j * P:(j + 1) * P, :].rearrange("a p n -> p (a n)")
                        dst = ring[:, SLOT[j], :]
                    else:
                        src = exp_w2[0, bass.ds(e, 1), (j - 8) * 2 * P:(j - 7) * 2 * P, :].rearrange(
                            "a (s p) n -> p (a s) n", p=P)
                        dst = ring[:, SLOT[j], :].rearrange("p (s n) -> p s n", s=2)
                    sp.dma_start(dst, src).then_inc(expert_in[j], 16)

            with sp.Fori(0, E) as e:
                load_expert(e, e)
            sp.wait_ge(rounds_in, 1)
            n_rounds = sp.value_load(rounds[0:1, 0:1], min_val=1, max_val=4)
            with sp.If(n_rounds > 1):
                with sp.Fori(1, n_rounds) as r:
                    with sp.Fori(0, E) as e:
                        load_expert(e, r * E + e)
            with sp.Else():
                sp.nop()
            for t in range(TT):
                sp.wait_ge(out_ready, t + 1)
                sp.dma_start(out[0, t * P:(t + 1) * P, :], HB[:, t, :]).then_inc(out_done, 16)
            sp.wait_ge(out_done, 16 * TT)

        @block.tensor
        def _(pe):
            mm = nc.tensor.matmul

            pe.wait_ge(const_in, 32)
            pe.wait_ge(xt_ready, 2)
            xs = ring[:, 11]
            for k in range(KT):
                if k >= 4:
                    pe.wait_ge(xn_ready, k - 3)
                for t in range(TT):
                    last = nc.tensor.transpose(ps[k % 4][:, t * P:(t + 1) * P],
                                               xs[:, t * D + k * P:t * D + (k + 1) * P], C("ident"))
                last.then_inc(xt_done, 1)

            def bank_free(b):
                if b < 4:
                    pe.wait_ge(xn_ready, KT)
                elif b - 4 < N_SHIFT:
                    pe.wait_ge(blk_shifted, b - 3)
                else:
                    pe.wait_ge(blk_copied, b - 3 - N_SHIFT)

            def project(b, n, c0, width):
                bank_free(b)
                s, v = chunk_in(n)
                pe.wait_ge(s, v)
                for k in range(KT):
                    last = mm(ps[b % 4][0:width, 0:T], chunk(n)[:, k, c0:c0 + width], XN[:, k, :],
                              start=k == 0, stop=k == KT - 1)
                last.then_inc(blk_done, 1)

            def head_sums(src, banks):
                for i, b in enumerate(banks):
                    last = mm(ps[b][:, :], C("head_ones"), src[:, 512 * i:512 * i + 512], start=True, stop=True)
                last.then_inc(pe_sum, 1)

            for b in range(N_SHIFT):
                n, c0, width = blocks[b]
                project(b, n, c0, width)
            pe.wait_ge(lora_in, 64)
            pe.wait_ge(lora_act, 3)
            b = N_SHIFT
            for kind in range(3):
                for m in range(KT):
                    bank_free(b)
                    o, cs = ps[b % 4][:, 0:T], slice(m * P, (m + 1) * P)
                    if kind == 0:
                        last = mm(o, flat(i_GB)[0:64, cs], CS[0:64, 0, :], start=True, stop=True)
                    elif kind == 1:
                        last = mm(o, flat(i_GB)[64:128, cs], CS[64:128, 0, :], start=True, stop=True)
                    else:
                        mm(o, flat(i_GB)[:, D + m * P:D + (m + 1) * P], CS[:, 1, :], start=True, stop=False)
                        last = mm(o, flat(i_XI)[0:32, cs], CS[0:32, 2, :], start=False, stop=True)
                    last.then_inc(blk_done, 1)
                    b += 1
            for i in range(N_SHIFT, len(blocks)):
                n, c0, width = blocks[i]
                project(b, n, c0, width)
                b += 1
                if i == N_SHIFT + 7:
                    pe.wait_ge(dve_step, 1)
                    head_sums(flat(i_TMP), (4, 5, 6, 7))
                if i == N_SHIFT + 23:
                    pe.wait_ge(dve_step, 4)
                    head_sums(flat(i_BON), (4, 5, 6, 7))

            pe.wait_ge(blk_done, len(blocks) + 3 * KT)
            pe.sem_inc(w_used, 2)

            pe.wait_ge(dve_step, 5)
            pe.wait_ge(blk_copied, len(blocks) + 24 - N_SHIFT)
            for g, (src, c) in enumerate([(V, 0), (V, 1), (AA, 0), (Kt, 0)]):
                for half in range(2):
                    for i in range(4):
                        last = nc.tensor.transpose(ps[2 * g + half][:, i * P:(i + 1) * P],
                                                   src[:, 4 * half + i, c * P:(c + 1) * P], C("ident"))
                    last.then_inc(pe_tok, 1)
            pe.wait_ge(act_tok, 8)

            U4 = lambda t, i: t[:, i * P:(i + 1) * P]
            Q4 = lambda t, i: t[:, i * HEAD:(i + 1) * HEAD]
            tok = lambda c: slice(c * P, (c + 1) * P)
            small = lambda t, i: t[0:64, i * P:i * P + 64]


            def four(c, bank, lhs, rhs):
                for i in range(4):
                    last = mm(ps[4 * c + bank][:, i * P:(i + 1) * P], lhs(i), rhs(i), start=True, stop=True)
                return last

            def head(arr_, bt, c):
                rows, m0 = slice(64 * (bt % 2), 64 * (bt % 2) + 64), 4 * (bt // 2)
                return lambda i: arr_[rows, m0 + i, tok(c)]

            u = lambda arr_, c: (lambda i: U4(arr_[:, c, :], i))

            def first(bt, c):
                if bt:
                    pe.wait_ge(dve_l[c], bt * ND)
                    pe.wait_ge(act_l[c], bt * NA)
                four(c, 0, head(AA, bt, c), head(KK, bt, c))
                four(c, 1, head(KK, bt, c), head(AA, bt, c)).then_inc(pe_l[c], 1)

            def second(bt, c):
                if bt:
                    pe.wait_ge(y_taken[c], bt)
                    if not c:
                        pe.wait_ge(s_taken, bt)
                four(c, 2, head(Kt, bt, c), head(KK, bt, c))
                four(c, 3, head(Kt, bt, c), head(R, bt, c)).then_inc(pe_l[c], 1)

            for c in range(2):
                first(0, c)
            second(0, 0)
            for bt in range(4):
                q, m0 = bt % 2, 4 * (bt // 2)
                rows = slice(64 * q, 64 * q + 64)
                hcol = lambda i: slice((m0 + i) * P + 64 * q, (m0 + i) * P + 64 * q + 64)
                if bt == 1:
                    pe.wait_ge(dve_step, 6)
                    pe.sem_inc(w_used, 1)
                pe.wait_ge(dve_l[0], bt * ND + 1)
                four(0, 0, head(AA, bt, 0), head(R, bt, 0)).then_inc(pe_l[0], 1)
                second(bt, 1)
                pe.wait_ge(dve_l[1], bt * ND + 1)
                four(1, 0, head(AA, bt, 1), head(R, bt, 1)).then_inc(pe_l[1], 1)
                for c in range(2):
                    pe.wait_ge(dve_l[c], bt * ND + 5)
                    four(c, 1, u(mAT, c), u(mA, c))
                    four(c, 2, u(mA, c), u(mAT, c)).then_inc(pe_l[c], 1)
                if bt == 2:
                    for c in range(2):
                        pe.wait_ge(y_taken[c], bt)
                        pe.wait_ge(dve_l[c], bt * ND + 7)
                    head_sums(flat(i_SW)[:, 0:1024], (0, 4))
                for c in range(2):
                    pe.wait_ge(act_l[c], bt * NA + 1)
                    pe.wait_ge(dve_l[c], bt * ND + 6)
                    four(c, 3, u(mP, c), u(mE, c)).then_inc(pe_l[c], 1)
                for c in range(2):
                    pe.wait_ge(act_l[c], bt * NA + 2)
                    four(c, 1, u(mPT, c), u(mP, c))
                    four(c, 2, u(mP, c), u(mPT, c)).then_inc(pe_l[c], 1)
                for c in range(2):
                    pe.wait_ge(act_l[c], bt * NA + 3)
                    pe.wait_ge(dve_l[c], bt * ND + 8)
                    four(c, 3, u(mA, c), u(mE, c)).then_inc(pe_l[c], 1)
                if bt == 2:
                    pe.wait_ge(y_centred, 1)
                    head_sums(yt, (0, 4))
                for c in range(2):
                    pe.wait_ge(act_l[c], bt * NA + 4)
                    four(c, 1, u(mAT, c), u(mA, c)).then_inc(pe_l[c], 1)
                for c in range(2):
                    pe.wait_ge(act_l[c], bt * NA + 5)
                    pe.wait_ge(dve_l[c], bt * ND + 9)
                    four(c, 3, u(mP, c), u(mE, c)).then_inc(pe_l[c], 1)
                if bt == 2:
                    pe.wait_ge(y_var, 1)
                def product_z(c):
                    if c:
                        pe.wait_ge(s_taken, bt + 1)
                    for i in range(4):
                        z = Q4(ps[4 * c + 3], i)
                        last = mm(z, U4(mAK[:, c, :], i), vtok[:, c, hcol(i)], start=True, stop=not c)
                        if c:
                            last = mm(z, KK[rows, m0 + i, tok(1)], st[rows, m0 + i, :], start=False, stop=True)
                    last.then_inc(z_done[c], 1)

                for lv in range(3):
                    for c in range(2):
                        pe.wait_ge(dve_l[c], bt * ND + 10 + 2 * lv)
                        for i in range(4):
                            if lv < 2:
                                last = nc.tensor.transpose(U4(ps[4 * c], i), U4(mE[:, c, :], i), C("ident"))
                            else:
                                last = nc.tensor.transpose(small(ps[4 * c], i), small(mE[:, c, :], i),
                                                           C("ident", 64)[0:64])
                        last.then_inc(pe_l[c], 1)
                    for c in range(2):
                        for i in range(4):
                            if lv < 2:
                                last = mm(U4(ps[4 * c + 1], i), U4(mL[:, c, :], i), U4(mE[:, c, :], i),
                                          start=True, stop=True)
                            else:
                                last = mm(small(ps[4 * c + 1], i), mL[64:128, c, i * P:i * P + 64],
                                          mE[64:128, c, i * P + 64:i * P + 128], start=True, stop=True)
                        last.then_inc(pe_l[c], 1)
                    if lv == 2:
                        product_z(0)
                    for c in range(2):
                        pe.wait_ge(act_l[c], bt * NA + 6 + lv)
                        pe.wait_ge(dve_l[c], bt * ND + 11 + 2 * lv)
                        for i in range(4):
                            cut = U4 if lv < 2 else small
                            last = mm(cut(ps[4 * c + 2], i), cut(mPT[:, c, :], i), cut(mP[:, c, :], i),
                                      start=True, stop=True)
                        last.then_inc(pe_l[c], 1)

                def product_u(c):
                    pe.wait_ge(z_taken[c], bt + 1)
                    for i in range(4):
                        last = mm(Q4(ps[4 * c + 3], 4 + i), U4(mE[:, c, :], i), Q4(zb[:, c, :], i), start=True, stop=True)
                    last.then_inc(u_made[c], 1)

                def product_y(c):
                    pe.wait_ge(u_taken[c], bt + 1)
                    pe.wait_ge(dve_l[c], bt * ND + 16)
                    for i in range(4):
                        o = ps[4 * c + 2][rows, i * P:(i + 1) * P]
                        mm(o, Q4(ub[:, c, :], i), U4(mRB[:, c, :], i), start=True, stop=False)
                        last = mm(o, vtok[:, c, hcol(i)], U4(mRK[:, c, :], i), start=False, stop=not c)
                        if c:
                            last = mm(o, st[rows, m0 + i, :], R[rows, m0 + i, tok(1)], start=False, stop=True)
                    last.then_inc(y_made[c], 1)

                pe.wait_ge(dve_l[0], bt * ND + 16)
                product_u(0)
                if bt < 3:
                    first(bt + 1, 0)
                pe.wait_ge(u_taken[0], bt + 1)
                for i in range(4):
                    o = ps[3][rows, i * HEAD:(i + 1) * HEAD]
                    mm(o, btok[:, hcol(i)], Q4(ub[:, 0, :], i), start=True, stop=False)
                    last = mm(o, ktok[:, hcol(i)], vtok[:, 0, hcol(i)], start=False, stop=True)
                last.then_inc(s_made, 1)
                product_y(0)
                product_z(1)
                if bt < 3:
                    first(bt + 1, 1)
                pe.wait_ge(dve_l[1], bt * ND + 16)
                product_u(1)
                if bt < 3:
                    second(bt + 1, 0)
                product_y(1)

            for c in range(2):
                pe.wait_ge(y_taken[c], 4)
            pe.sem_inc(w_used, 5)
            head_sums(flat(i_SW)[:, 1024:2048], (4, 5))

            def out_product(t, half, k0, n=4):
                s, v = chunk_in(NIN + half)
                pe.wait_ge(s, v)
                for k in range(k0, k0 + n):
                    last = mm(ps[2 * t + half][:, :], Y[:, k, t * P:(t + 1) * P], chunk(NIN + half)[:, k, :],
                              start=k == 0, stop=k == KT - 1)
                return last

            pe.wait_ge(merged, 1)
            pe.wait_ge(s_taken, 4)
            out_product(0, 0, 0)
            pe.wait_ge(y_centred, 2)
            head_sums(yt, (6, 7))
            out_product(0, 1, 0)
            for half in range(2):
                out_product(1, half, 0)
            for t in range(TT):
                for k0 in (4, 6):
                    pe.wait_ge(merged, 2 + (k0 - 4) // 2)
                    for half in range(2):
                        last = out_product(t, half, k0, 2)
                last.then_inc(wout_done, 1)
            pe.wait_ge(wout_done, TT)
            pe.sem_inc(w_used, 4)
            for t in range(TT):
                pe.wait_ge(dve_h, 2 + 2 * t)
                for k in range(KT):
                    last = nc.tensor.transpose(ps[4 + 2 * t + k // 4][:, (k % 4) * P:(k % 4) * P + P],
                                               HN[:, t, k * P:(k + 1) * P], C("ident"))
                    if k % 4 == 3:
                        last.then_inc(pe_h, 1)
            pe.wait_ge(late_in, 16 * 4)
            for t in range(TT):
                pe.wait_ge(act_h, 2 + 2 * t + 2)
                for k in range(KT):
                    last = mm(ps[t][:, 0:E], HNT[:, k, t * P:(t + 1) * P], rw[:, k, :],
                              start=k == 0, stop=k == KT - 1)
                last.then_inc(pe_h, 1)
            pe.wait_ge(dve_h, 6)
            mm(ps[7][:, 0:E], C("above"), msk[:, 0, :], start=True, stop=True)
            mm(ps[7][:, E:2 * E], C("ones"), msk[:, 0, :], start=True, stop=False)
            mm(ps[7][:, E:2 * E], C("above"), msk[:, 1, :], start=False, stop=True)
            mm(ps[7][:, 2 * E:3 * E], C("ones"), msk[:, 0, :], start=True, stop=False)
            mm(ps[7][:, 2 * E:3 * E], C("ones"), msk[:, 1, :], start=False, stop=True)
            pe.wait_ge(dve_h, 7)
            for t in range(TT):
                last = nc.tensor.transpose(ps[5][0:E, t * P:(t + 1) * P], gw[:, t, 0:E], C("ident"))
            last.then_inc(pe_h, 1)

            def gather():
                for k in range(KT):
                    for t in range(TT):
                        for s in range(3):
                            last = mm(ps[6][:, k * CAP:(k + 1) * CAP], H3[:, t, s, k * P:(k + 1) * P],
                                      sel[:, t, :], start=t + s == 0, stop=t + s == 3)
                last.then_inc(gathered, 1)

            def turn_gates():
                for t in range(TT):
                    last = nc.tensor.transpose(ps[7][:, t * P:(t + 1) * P], gsel[:, t, :], C("ident"))
                last.then_inc(gate_turned, 1)

            pe.wait_ge(gates_copied, 1)
            for t in range(TT):
                for half in range(2):
                    mm(ps[2 * t + half][:, :], gwT[:, t * P:(t + 1) * P], b2s[0:E, half * 512:half * 512 + 512],
                       start=True, stop=True)
            pe.wait_ge(sel_ready, 4)
            pe.wait_ge(h3_cast, 3 * TT)
            gather()
            turn_gates()

            n_rounds = pe.value_load(rounds[0:1, 0:1], min_val=1, max_val=4)
            with pe.Fori(0, n_rounds) as r:
                with pe.Fori(0, E) as e:
                    it = r * E + e
                    pe.wait_ge(u_free, it + 1)
                    for part in range(2):
                        for half in range(2):
                            last = mm(ps[4 + part][64 * half:64 * half + 64, :], oh[:, :],
                                      b1s[0:3 * E, part * D + half * 512:part * D + half * 512 + 512],
                                      start=True, stop=False)
                    last.then_inc(b1_used, 1)
                    pe.wait_ge(xe_ready, it + 1)
                    for k in range(8):
                        pe.wait_ge(expert_in[k], (it + 1) * 16)
                        for part in range(2):
                            for half in range(2):
                                last = mm(ps[4 + part][64 * half:64 * half + 64, :], xe[:, k * CAP:(k + 1) * CAP],
                                          ring[:, SLOT[k], part * D + half * 512:part * D + half * 512 + 512],
                                          start=False, stop=k == 7)
                        last.then_inc(w_used, 1)
                    pe.wait_ge(act_ready, it + 1)
                    for c in range(4):
                        last = nc.tensor.transpose(ps[6][:, c * P:(c + 1) * P], actb[:, c * P:(c + 1) * P], C("ident"))
                    last.then_inc(act_turned, 1)
                    pe.wait_ge(gt_ready, it + 1)
                    pe.wait_ge(at_ready, it + 1)
                    for j in range(4):
                        pe.wait_ge(expert_in[8 + j], (it + 1) * 16)
                        for i in range(2):
                            k = 2 * j + i
                            lhs = actT[:, (k % 4) * P + (k // 4) * CAP:(k % 4) * P + (k // 4) * CAP + CAP]
                            for half in range(2):
                                last = mm(ps[7][64 * half:64 * half + 64, :], lhs,
                                          ring[:, SLOT[8 + j], i * D + half * 512:i * D + half * 512 + 512],
                                          start=k == 0, stop=k == 7)
                        last.then_inc(w_used, 1)
                    pe.wait_ge(sel_ready, (it + 2) * 4)
                    gather()
                    pe.wait_ge(y_ready, it + 1)
                    for t in range(TT):
                        for half in range(2):
                            last = mm(ps[2 * t + half][:, :], gts[64 * half:64 * half + 64, t * P:(t + 1) * P],
                                      yb[64 * half:64 * half + 64, :], start=False, stop=False, skip_group_check=True)
                    last.then_inc(combined, 1)
                    turn_gates()

        @block.scalar
        def _(act):
            af = nc.scalar.activation
            for t in range(TT):
                act.wait_ge(x_in[t], 16)
                af(flat(i_SW)[:, 0:D], flat(i_G2)[:, t * D:(t + 1) * D], ACT.Square,
                   accum_out=col[:, t:t + 1]).then_inc(act_rms, 1)
                act.wait_ge(act_rms, t + 1)
            act.wait_ge(dve_rms, 1)
            af(col[:, 4:6], col[:, 2:4], ACT.Sqrt).then_inc(act_rms, 1)
            for k in range(KT):
                act.wait_ge(xt_done, k + 1)
                af(XN[:, k, :], ps[k % 4][:, 0:T], ACT.Copy, scale=pc("norm_mix_g", k)).then_inc(xn_ready, 1)
            act.wait_ge(dve_rms, 3)
            for b in range(N_SHIFT):
                h = blocks[b][2]
                act.wait_ge(blk_done, b + 1)
                af(shifted(b), ps[b % 4][0:h, 0:T], ACT.Copy, scale=inv[0:h, b:b + 1]).then_inc(blk_scaled, 1)
                if b == 2:
                    act.wait_ge(blk_shifted, 3)
                    af(CS[0:64, 0, :], CS[0:64, 0, :], ACT.Tanh).then_inc(lora_act, 1)
                    af(CS[:, 1, :], CS[:, 1, :], ACT.Sigmoid).then_inc(lora_act, 1)
                    af(CS[0:32, 2, :], CS[0:32, 2, :], ACT.Sigmoid).then_inc(lora_act, 1)
            act.wait_ge(dve_rms, 2)
            act.wait_ge(xt_done, KT)
            b = N_SHIFT
            for kind, dst in enumerate((SW, AA, G, GC, XI, GB, G1, G2)):
                for m in range(KT):
                    act.wait_ge(blk_done, b + 1)
                    o, i = dst[:, m, :], ps[b % 4][:, 0:T]
                    if kind == 0:
                        af(o, i, ACT.Sigmoid, bias=pc("w0", m)).then_inc(blk_copied, 1)
                    elif kind == 1:
                        af(o, i, ACT.Sigmoid, bias=pc("a0", m)).then_inc(blk_copied, 1)
                    elif kind < 6:
                        af(o, i, ACT.Copy).then_inc(blk_copied, 1)
                    else:
                        af(o, i, ACT.Sigmoid).then_inc(blk_copied, 1)
                    b += 1
                if kind == 3:
                    act.wait_ge(dve_step, 2)
                    af(flat(i_TMP), flat(i_TMP), ACT.Sqrt).then_inc(act_step, 1)
                if kind == 4:
                    act.wait_ge(dve_step, 3)
                    af(flat(i_SW), flat(i_SW), ACT.Exp, scale=-KAPPA).then_inc(act_step, 1)
                    af(flat(i_TMP), flat(i_CS), ACT.Exp, scale=-KAPPA).then_inc(act_step, 1)
                    act.wait_ge(act_step, 3)
                    af(flat(i_CS), flat(i_CS), ACT.Exp, scale=KAPPA).then_inc(act_step, 1)
                    af(dec[:], dec[:], ACT.Exp, scale=-KAPPA).then_inc(act_step, 1)
            for n in range(8):
                dst = (vtok[:, 0], vtok[:, 1], btok[:], ktok[:])[n // 2][:, 512 * (n % 2):512 * (n % 2) + 512]
                act.wait_ge(pe_tok, n + 1)
                af(dst, ps[n][:, :], ACT.Copy).then_inc(act_tok, 1)
            def root(half):
                act.wait_ge(y_var, half + 1)
                af(yt, yt, ACT.Sqrt).then_inc(y_root, 1)

            act.wait_ge(dve_step, 6)
            for bt in range(4):
                if bt == 1:
                    act.wait_ge(factors_ready, 1)
                    for s in range(3):
                        act.dma_start(b1f[E * s:E * s + E, :], exp_b1[0]).then_inc(b1_in, 16)
                q, m0 = bt % 2, 4 * (bt // 2)
                rows = slice(64 * q, 64 * q + 64)
                n_pe = lambda c, k: bt * NPE + k

                def take(c, k, dst, bank):
                    act.wait_ge(pe_l[c], n_pe(c, k))
                    af(dst[:, c, :], ps[4 * c + bank][:, :], ACT.Copy).then_inc(act_l[c], 1)

                def take_z(c):
                    act.wait_ge(z_done[c], bt + 1)
                    af(zb[:, c, :], ps[4 * c + 3][:, 0:4 * HEAD], ACT.Copy).then_inc(z_taken[c], 1)

                for k, first, second in ((4, mP, mPT), (6, mA, mAT)):
                    for c in range(2):
                        take(c, k, first, 1)
                        take(c, k, second, 2)
                for c in range(2):
                    act.wait_ge(pe_l[c], n_pe(c, 7))
                    take(c, 8, mP, 1)
                for lv in range(3):
                    for c in range(2):
                        if lv < 2:
                            take(c, 10 + 3 * lv, mPT, 0)
                        else:
                            act.wait_ge(pe_l[c], n_pe(c, 10 + 3 * lv))
                            quarter = lambda t: t[0:64, :].rearrange("p (i n) -> p i n", i=4)[:, :, 0:64]
                            af(quarter(mPT[:, c, :]), quarter(ps[4 * c]), ACT.Copy).then_inc(act_l[c], 1)
                    if bt == 2 and lv == 0:
                        root(0)
                    if lv == 2:
                        take_z(0)
                for c in range(2):
                    if c:
                        take_z(1)
                    act.wait_ge(u_made[c], bt + 1)
                    af(ub[:, c, :], ps[4 * c + 3][:, 4 * HEAD:8 * HEAD], ACT.Copy).then_inc(u_taken[c], 1)
                    act.wait_ge(y_made[c], bt + 1)
                    af(Y[rows, m0:m0 + 4, c * P:(c + 1) * P],
                       ps[4 * c + 2][rows, :].rearrange("p (m t) -> p m t", m=4), ACT.Copy).then_inc(y_taken[c], 1)
            act.wait_ge(w_used, 8)
            for t in range(TT):
                act.dma_start(HB[:, t, :], x[0, t * P:(t + 1) * P, :]).then_inc(xres_in, 16)
            act.dma_start(rw, router_w[0].rearrange("(k p) e -> p k e", p=P)).then_inc(late_in, 16)
            act.dma_start(rb, router_b[0:1, :].partition_broadcast(P)).then_inc(late_in, 16)
            root(1)
            act.wait_ge(merged, 3)
            act.dma_start(gffn, norm_ffn_g[0:1, :].partition_broadcast(P)).then_inc(gffn_in, 16)
            act.dma_start(gfin, norm_final_g.partition_broadcast(P)).then_inc(late_in, 16)
            act.dma_start(b2s[0:E, :], exp_b2[0]).then_inc(late_in, 16)

            def root_of_squares(t, src, dst, ready, n, signal):
                act.wait_ge(ready, n)
                af(HN[:, t, :], HB[:, t, :], ACT.Square, accum_out=col[:, src + t:src + t + 1]).then_inc(act_chain, 1)
                squares[0] += 1
                act.wait_ge(act_chain, squares[0])
                af(col[:, dst + t:dst + t + 1], col[:, src + t:src + t + 1], ACT.Sqrt, scale=1.0 / D,
                   bias=col[:, 30:31]).then_inc(signal, 1)

            squares = [0]
            for t in range(TT):
                root_of_squares(t, 8, 12, dve_h, 1 + 2 * t, act_h)
            def part(s_, t):
                if s_ == 0:
                    act.wait_ge(dve_h, 2 + 2 * t)
                else:
                    act.wait_ge(h3_left, 2 * (s_ - 1) + t + 1)
                af(H3[:, t, s_, :], HN[:, t, :] if s_ == 0 else h3tmp[t], ACT.Copy).then_inc(h3_cast, 1)

            for t in range(TT):
                for half in range(2):
                    act.wait_ge(pe_h, 2 * t + half + 1)
                    af(HNT[:, 4 * half:4 * half + 4, t * P:(t + 1) * P],
                       ps[4 + 2 * t + half][:, :].rearrange("p (k n) -> p k n", k=4), ACT.Copy).then_inc(act_h, 1)
                part(0, t)
            for t in range(TT):
                part(1, t)
            act.wait_ge(dve_h, 5)
            af(ge[:, :, 0:TOP], ge[:, :, 0:TOP], ACT.Exp).then_inc(act_h, 1)
            for t in range(TT):
                part(2, t)

            act.wait_ge(gathered, 1)
            af(xe, ps[6][:, :], ACT.Copy).then_inc(xe_ready, 1)
            act.wait_ge(rounds_in, 1)
            n_rounds = act.value_load(rounds[0:1, 0:1], min_val=1, max_val=4)
            with act.Fori(0, n_rounds) as r:
                with act.Fori(0, E) as e:
                    it = r * E + e
                    act.wait_ge(glu_ready, it + 1)
                    af(sig, glu, ACT.Sigmoid, scale=ALPHA).then_inc(sig_ready, 1)
                    act.wait_ge(act_turned, it + 1)
                    af(actT, ps[6][:, :], ACT.Copy).then_inc(at_ready, 1)
                    act.wait_ge(gathered, it + 2)
                    af(xe, ps[6][:, :], ACT.Copy).then_inc(xe_ready, 1)
            for t in range(TT):
                root_of_squares(t, 16, 20, dve_h, 8 + t, act_h)

        @block.gpsimd
        def _(pool):
            for s_ in range(2):
                for t in range(TT):
                    pool.wait_ge(h3_cast, 2 * s_ + t + 1)
                    nc.gpsimd.tensor_tensor(h3tmp[t], HN[:, t, :] if s_ == 0 else h3tmp[t], H3[:, t, s_, :],
                                            ALU.subtract).then_inc(h3_left, 1)

        @block.vector
        def _(v):
            tt, ts, stt, cp = nc.vector.tensor_tensor, nc.vector.tensor_scalar, nc.vector.scalar_tensor_tensor, nc.vector.tensor_copy
            linked = [0]

            def link(ins):
                linked[0] += 1
                ins.then_inc(dve_chain, 1)
                v.wait_ge(dve_chain, linked[0])

            def per_feature(name, n=T):
                return par[:, P_AT[name]:P_AT[name] + KT].unsqueeze(2).to_broadcast([P, KT, n])

            def root_mean(src, dst, signal):
                ts(col[:, dst:dst + 2], col[:, src:src + 2], 1.0 / D, NORM_EPS, ALU.mult, ALU.add).then_inc(signal, 1)

            nc.vector.memset(col[:, 30:31], NORM_EPS)
            v.wait_ge(act_rms, 2)
            root_mean(0, 2, dve_rms)
            v.wait_ge(act_rms, 3)
            link(nc.vector.reciprocal(col[:, 6:8], col[:, 4:6]))
            for t in range(TT):
                last = ts(ring[:, 11, t * D:(t + 1) * D], flat(i_G2)[:, t * D:(t + 1) * D], col[:, 6 + t:7 + t], None, ALU.mult)
                last.then_inc(xt_ready, 1)
            v.wait_ge(xt_ready, 2)
            v.sem_inc(dve_rms, 1)
            v.wait_ge(const_in, 32)
            link(ts(inv[:, 0:3], par[:, P_AT["mu_lora"]:P_AT["mu_lora"] + 3], -1.0, 1.0, ALU.mult, ALU.add))
            for i, n in enumerate(("mu_k", "mu_r", "mu_v", "k_a")):
                link(ts(inv[:, 3 + 8 * i:11 + 8 * i], par[:, P_AT[n]:P_AT[n] + 8], -1.0, 1.0, ALU.mult, ALU.add))
            v.sem_inc(dve_rms, 1)
            for b in range(N_SHIFT):
                h = blocks[b][2]
                mu = pc("mu_lora", b, h) if b < 3 else pc(("mu_k", "mu_r", "mu_v")[(b - 3) // 8], (b - 3) % 8)
                v.wait_ge(blk_scaled, b + 1)
                o = shifted(b)
                stt(o[:, 1:T], ps[b % 4][0:h, 0:T - 1], mu, o[:, 1:T], ALU.mult, ALU.add).then_inc(blk_shifted, 1)
            v.wait_ge(blk_shifted, N_SHIFT)
            link(tt(KK, Kt, per_feature("k_k"), ALU.mult))
            tt(TMP, KK, KK, ALU.mult).then_inc(dve_step, 1)
            v.wait_ge(blk_copied, 3 * KT)
            link(nc.vector.memset(flat(i_BON), 1.0))
            link(nc.vector.memset(flat(i_BON).rearrange("p (c t) -> p c t", t=P)[:, :, 0:1], 0.0))
            link(nc.vector.tensor_tensor_scan(flat(i_CS), flat(i_BON), flat(i_SW), 0.0, ALU.mult, ALU.add))
            cs4 = flat(i_CS).rearrange("p (m c t) -> p m c t", m=KT, c=TT)
            link(cp(cm[:], cs4[:, :, :, HEAD - 1]))
            link(cp(ce[:], cs4[:, :, :, P - 1]))
            link(tt(dec[:], ce[:, :, 0], cm[:, :, 0], ALU.subtract))
            link(tt(dec[:], dec[:], cm[:, :, 1], ALU.add))
            cs3 = flat(i_CS).rearrange("p (c t) -> p c t", t=P)
            link(tt(cs3, cs3, cm[:].rearrange("p m c -> p (m c)").unsqueeze(2).to_broadcast([P, 2 * KT, P]), ALU.subtract))
            link(tt(SW, CS, SW, ALU.subtract))
            v.wait_ge(pe_sum, 1)
            for i in range(4):
                last = ts(flat(i_TMP)[:, 512 * i:512 * i + 512], ps[4 + i][:, :], 1e-24, None, ALU.max)
            link(last)
            v.sem_inc(dve_step, 1)
            v.wait_ge(act_step, 1)
            link(nc.vector.reciprocal(flat(i_TMP), flat(i_TMP)))
            link(tt(KK, KK, TMP, ALU.mult))
            v.sem_inc(dve_step, 1)
            link(tt(BON, AA, per_feature("k_a"), ALU.mult))
            link(tt(BON, BON, inv[:, 27:35].unsqueeze(2).to_broadcast([P, KT, T]), ALU.add))
            link(tt(Kt, Kt, BON, ALU.mult))
            link(tt(AA, KK, AA, ALU.mult))
            link(tt(BON, R, Kt, ALU.mult))
            link(tt(BON, BON, per_feature("r_k"), ALU.mult))
            v.sem_inc(dve_step, 1)
            v.wait_ge(act_step, 5)
            link(stt(flat_ring(7), flat_ring(7), -1.0, flat(i_SW), ALU.mult, ALU.mult))
            link(tt(R, R, TMP, ALU.mult))
            link(tt(AA, AA, CS, ALU.mult))
            link(tt(Kt, Kt, CS, ALU.mult))
            v.wait_ge(pe_sum, 2)
            for i in range(4):
                s_ = slice(512 * i, 512 * i + 512)
                last = tt(flat(i_BON)[:, s_], ps[4 + i][:, :], flat_ring(10)[:, s_], ALU.mult)
            link(last)
            v.sem_inc(dve_step, 1)
            v.wait_ge(blk_copied, 5 * KT)
            link(tt(GC, GC, XI, ALU.mult))
            link(tt(XI, GC, per_feature("conv2"), ALU.mult))
            for back, name in ((1, "conv1"), (2, "conv0")):
                for m in range(KT):
                    last = stt(XI[:, m, back:], GC[:, m, 0:T - back], pc(name, m), XI[:, m, back:], ALU.mult, ALU.add)
                link(last)
            v.wait_ge(blk_copied, 6 * KT)
            link(tt(XI, XI, GB, ALU.mult))
            v.wait_ge(blk_copied, 7 * KT)
            link(tt(XI, XI, G1, ALU.mult))
            v.sem_inc(dve_step, 1)
            v.wait_ge(blk_copied, 8 * KT)

            def factors(step):
                if step == 0:
                    link(tt(G, G, G2, ALU.mult))
                if step == 1:
                    link(tt(BON, BON, per_feature("ln_b"), ALU.add))
                if step == 2:
                    link(tt(BON, BON, G, ALU.mult))
                if step == 3:
                    link(tt(BON, BON, XI, ALU.add))
                if step == 4:
                    link(tt(G, G, per_feature("ln_g"), ALU.mult))
                    v.sem_inc(factors_ready, 1)

            def split_b1(step):
                nb = 3 * E
                if step == 0:
                    v.wait_ge(b1_in, 48)
                    link(cp(b1s[0:nb, :], b1f[0:nb, :]))
                if step == 1:
                    link(tt(b1f[0:nb, :], b1f[0:nb, :], b1s[0:nb, :], ALU.subtract))
                if step == 2:
                    link(cp(b1m, b1f[0:nb, :]))
                    link(cp(b1s[E:2 * E, :], b1m[E:2 * E, :]))
                if step == 3:
                    link(tt(b1f[2 * E:nb, :], b1f[2 * E:nb, :], b1m[2 * E:nb, :], ALU.subtract))
                if step == 4:
                    link(cp(b1s[2 * E:nb, :], b1f[2 * E:nb, :]))

            ys = lambda half: flat(i_SW)[:, 1024 * half:1024 * half + 1024]

            def centre(half, banks):
                v.wait_ge(pe_sum, 3 + 2 * half)
                for i, b in enumerate(banks):
                    s_ = slice(512 * i, 512 * i + 512)
                    last = stt(ys(half)[:, s_], ps[b][:, :], -1.0 / HEAD, ys(half)[:, s_], ALU.mult, ALU.add)
                link(last)
                link(tt(yt, ys(half), ys(half), ALU.mult))
                v.sem_inc(y_centred, 1)

            def variance(half, banks):
                v.wait_ge(pe_sum, 4 + 2 * half)
                for i, b in enumerate(banks):
                    last = ts(yt[:, 512 * i:512 * i + 512], ps[b][:, :], 1.0 / HEAD, GN_EPS, ALU.mult, ALU.add)
                link(last)
                v.sem_inc(y_var, 1)

            def merge(half, step, c0=0, width=1024):
                cut = slice(1024 * half + c0, 1024 * half + c0 + width)
                y_, dev = flat(i_SW)[:, cut], yt[:, c0:c0 + width]
                if step == 0:
                    if c0 == 0:
                        v.wait_ge(y_root, half + 1)
                    link(nc.vector.reciprocal(dev, dev))
                if step == 1:
                    link(tt(y_, y_, dev, ALU.mult))
                if step == 2:
                    link(tt(y_, y_, flat(i_G)[:, cut], ALU.mult))
                if step == 3:
                    link(tt(y_, y_, flat(i_BON)[:, cut], ALU.add))
                    v.sem_inc(merged, 1)

            b4 = lambda t: t.rearrange("p (i n) -> p i n", i=4)
            mask = lambda n: C(n).unsqueeze(1).to_broadcast([P, 4, P])
            def mask_first(bt, c):
                v.wait_ge(pe_l[c], bt * NPE + 1)
                for dst, bank, name in ((mAT, 0, "above16"), (mA, 1, "below16"), (mL, 1, "below")):
                    tt(b4(dst[:, c, :]), b4(ps[4 * c + bank][:, :]), mask(name), ALU.mult).then_inc(dve_l[c], 1)

            def first_e(bt, c):
                if bt:
                    v.wait_ge(u_made[c], bt)
                v.wait_ge(dve_l[c], bt * ND + 1)
                tt(b4(mE[:, c, :]), b4(mAT[:, c, :]), mask("ident"), ALU.add).then_inc(dve_l[c], 1)

            def mask_second(bt, c):
                v.wait_ge(pe_l[c], bt * NPE + 2)
                if bt:
                    v.wait_ge(y_made[c], bt)
                tt(b4(mAK[:, c, :]), b4(ps[4 * c + 2][:, :]), mask("above"), ALU.mult).then_inc(dve_l[c], 1)
                tt(b4(mRK[:, c, :]), b4(ps[4 * c + 3][:, :]), mask("above_eq"), ALU.mult).then_inc(dve_l[c], 1)

            for c in range(2):
                mask_first(0, c)
                first_e(0, c)
            mask_second(0, 0)
            for bt in range(4):
                q, m0 = bt % 2, 4 * (bt // 2)
                rows = slice(64 * q, 64 * q + 64)

                def at(c, k):
                    v.wait_ge(pe_l[c], bt * NPE + k)

                def done(c, ins):
                    ins.then_inc(dve_l[c], 1)

                def own(c, k):
                    v.wait_ge(dve_l[c], bt * ND + k)

                for c in range(2):
                    if c:
                        mask_second(bt, 1)
                    at(c, 3)
                    done(c, tt(b4(mRB[:, c, :]), b4(ps[4 * c][:, :]), mask("above_eq"), ALU.mult))
                for i, (k, n) in enumerate(((5, 4), (7, 8), (9, 9))):
                    for c in range(2):
                        at(c, k)
                        own(c, n)
                        done(c, tt(mE[:, c, :], mE[:, c, :], ps[4 * c + 3][:, :], ALU.add))
                    if bt == 0:
                        factors(i)
                    if bt == 1:
                        split_b1(i)
                    if bt == 2 and i == 0:
                        centre(0, (0, 4))
                    if bt == 2 and i == 2:
                        variance(0, (0, 4))
                    if bt == 3:
                        merge(0, i)
                for lv in range(3):
                    for c in range(2):
                        at(c, 11 + 3 * lv)
                        if lv < 2:
                            done(c, tt(b4(mP[:, c, :]), b4(ps[4 * c + 1][:, :]), mask(("pair16", "pair32")[lv]), ALU.mult))
                        else:
                            done(c, cp(b4(mP[0:64, c, :])[:, :, 0:64], b4(ps[4 * c + 1][0:64, :])[:, :, 0:64]))
                    for c in range(2):
                        at(c, 12 + 3 * lv)
                        own(c, 10 + 2 * lv)
                        if lv < 2:
                            done(c, tt(mE[:, c, :], mE[:, c, :], ps[4 * c + 2][:, :], ALU.add))
                        else:
                            done(c, cp(b4(mE[0:64, c, :])[:, :, 64:128], b4(ps[4 * c + 2][0:64, :])[:, :, 0:64]))
                    if bt == 0 and lv < 2:
                        factors(3 + lv)
                    if bt == 1 and lv < 2:
                        split_b1(3 + lv)
                    if bt == 3 and lv == 0:
                        merge(0, 3)
                v.wait_ge(s_made, bt + 1)
                tt(st[rows, m0:m0 + 4, :], ps[3][rows, 0:4 * HEAD].rearrange("p (m n) -> p m n", m=4),
                   dec[rows, m0:m0 + 4].unsqueeze(2).to_broadcast([64, 4, HEAD]), ALU.mult).then_inc(s_taken, 1)
                if bt < 3:
                    mask_first(bt + 1, 0)
                    first_e(bt + 1, 0)
                    mask_first(bt + 1, 1)
                    first_e(bt + 1, 1)
                    mask_second(bt + 1, 0)
            centre(1, (4, 5))
            variance(1, (6, 7))
            for c0 in (0, 512):
                for step in range(4):
                    merge(1, step, c0, 512)
            for t in range(TT):
                v.wait_ge(wout_done, t + 1)
                v.wait_ge(xres_in, 16 * TT)
                for half in range(2):
                    s_ = slice(512 * half, 512 * half + 512)
                    last = tt(HB[:, t, s_], HB[:, t, s_], ps[2 * t + half][:, :], ALU.add)
                last.then_inc(dve_h, 1)
                v.wait_ge(gffn_in, 16)
                v.wait_ge(act_h, t + 1)
                link(nc.vector.reciprocal(col[:, 14 + t:15 + t], col[:, 12 + t:13 + t]))
                stt(HN[:, t, :], HB[:, t, :], col[:, 14 + t:15 + t], gffn, ALU.mult, ALU.mult).then_inc(dve_h, 1)
            for t in range(TT):
                v.wait_ge(pe_h, 5 + t)
                link(tt(lg[:, t, :], ps[t][:, 0:E], rb, ALU.add))
                link(nc.vector.max(mx[:, t, :], lg[:, t, :]))
                link(nc.vector.max_index(mi[:, t, :], mx[:, t, :], lg[:, t, :]))
            link(cp(mif[:], mi[:]))
            link(tt(ge[:, :, 0:TOP], mx[:, :, 0:TOP], mx[:, :, 0:1].to_broadcast([P, TT, TOP]), ALU.subtract))
            v.sem_inc(dve_h, 1)
            for t in range(TT):
                link(tt(hot[:, t], C("expert", E).unsqueeze(2).to_broadcast([P, E, TOP]),
                        mif[:, t, 0:TOP].unsqueeze(1).to_broadcast([P, E, TOP]), ALU.is_equal))
            link(nc.vector.tensor_reduce(msk[:], hot, AX_X, ALU.add))
            v.sem_inc(dve_h, 1)
            v.wait_ge(act_h, 7)
            link(nc.vector.tensor_reduce(cnt[:, 0:TT], ge[:, :, 0:TOP], AX_X, ALU.add))
            link(nc.vector.reciprocal(cnt[:, 2:2 + TT], cnt[:, 0:TT]))
            link(tt(ge[:, :, 0:TOP], ge[:, :, 0:TOP], cnt[:, 2:2 + TT].unsqueeze(2).to_broadcast([P, TT, TOP]), ALU.mult))
            for t in range(TT):
                link(tt(hot[:, t], hot[:, t], ge[:, t, 0:TOP].unsqueeze(1).to_broadcast([P, E, TOP]), ALU.mult))
            link(nc.vector.tensor_reduce(gw[:, :, 0:E], hot, AX_X, ALU.add))
            link(cp(gw[:, :, E:E + 1], gw[:, :, 0:1]))
            v.sem_inc(dve_h, 1)
            v.wait_ge(pe_h, 7)
            cp(gwT, ps[5][0:E, 0:T]).then_inc(gates_copied, 1)
            link(ts(rk[:, :, 0:E], msk[:], -FAR, FAR, ALU.mult, ALU.add))
            link(tt(rk[:, :, 0:E], rk[:, :, 0:E], ps[7][:, 0:2 * E].rearrange("p (t e) -> p t e", t=TT), ALU.add))
            link(ts(rk[:, :, E:E + 1], rk[:, :, 0:1], -float(CAP), None, ALU.add))
            link(nc.vector.tensor_reduce(cnt[:, 4:5], ps[7][:, 2 * E:3 * E], AX_X, ALU.max))
            link(ts(cnt[:, 5:6], cnt[:, 4:5], float(CAP), 1.0, ALU.is_gt, ALU.add))
            for n in range(2, T // CAP):
                link(stt(cnt[:, 5:6], cnt[:, 4:5], float(n * CAP), cnt[:, 5:6], ALU.is_gt, ALU.add))
            link(cp(rounds[:], cnt[:, 5:6]))
            v.sem_inc(rounds_in, 1)
            n_rounds = v.value_load(rounds[0:1, 0:1], min_val=1, max_val=4)
            v.sem_inc(u_free, 1)

            def select(e):
                tt(sel[:], C("slot", CAP).unsqueeze(1).to_broadcast([P, TT, CAP]),
                   rk[:, :, bass.ds(e, 1)].to_broadcast([P, TT, CAP]), ALU.is_equal).then_inc(sel_ready, 1)
                for t in range(TT):
                    ts(gsel[:, t, :], C("slot"), rk[:, t, bass.ds(e, 1)], gw[:, t, bass.ds(e, 1)],
                       ALU.is_equal, ALU.mult).then_inc(sel_ready, 1)
                ts(oh[:], C("ones", CAP)[0:3 * E], cst[0:3 * E, bass.ds(e + C_AT["pick"], 1)], None,
                   ALU.mult).then_inc(sel_ready, 1)

            select(0)
            with v.Fori(0, n_rounds) as r:
                with v.Fori(0, E) as e:
                    it = r * E + e
                    v.wait_ge(gate_turned, it + 1)
                    cp(gts[:, 0:T], ps[7][:, 0:T]).then_inc(gt_ready, 1)
                    v.wait_ge(w_used, it * 12 + 20)
                    ts(glu, ps[4][:, :], LIMIT, None, ALU.min).then_inc(glu_ready, 1)
                    ts(lin, ps[5][:, :], LIMIT, -LIMIT, ALU.min, ALU.max).then_inc(u_free, 1)
                    v.wait_ge(u_free, it + 2)
                    v.wait_ge(glu_ready, it + 1)
                    stt(lin, lin, 1.0, glu, ALU.add, ALU.mult).then_inc(lin_ready, 1)
                    v.wait_ge(sig_ready, it + 1)
                    v.wait_ge(lin_ready, it + 1)
                    tt(actb, lin, sig, ALU.mult).then_inc(act_ready, 1)
                    select(e + 1)
                    v.wait_ge(w_used, it * 12 + 24)
                    cp(yb, ps[7][:, :]).then_inc(y_ready, 1)
                v.wait_ge(sel_ready, (r + 1) * (4 * E) + 4)
                ts(rk[:], rk[:], -float(CAP), None, ALU.add).then_inc(round_ready, 1)
                v.wait_ge(round_ready, r + 1)
            v.wait_ge(combined, n_rounds * E)
            for t in range(TT):
                for half in range(2):
                    s_ = slice(512 * half, 512 * half + 512)
                    last = tt(HB[:, t, s_], HB[:, t, s_], ps[2 * t + half][:, :], ALU.add)
                last.then_inc(dve_h, 1)
            for t in range(TT):
                v.wait_ge(act_h, 8 + t)
                link(nc.vector.reciprocal(col[:, 22 + t:23 + t], col[:, 20 + t:21 + t]))
                stt(HB[:, t, :], HB[:, t, :], col[:, 22 + t:23 + t], gfin, ALU.mult, ALU.mult).then_inc(out_ready, 1)


_DIRECT = ["x", "w_in", "w_out", "norm_ffn_g", "norm_final_g", "decay_w2", "iclr_a2", "gate_g2", "router_w",
           "router_b", "exp_w1", "exp_b1", "exp_w2", "exp_b2"]


def kernel(**inputs):
    import concourse.bacc as bacc
    from concourse.bass_utils import run_bass_kernel_spmd

    nc = bacc.Bacc("TRN2", target_bir_lowering=False, num_devices=1)
    arrays = {n: np.ascontiguousarray(inputs[n]) for n in _DIRECT}
    mu = np.asarray(inputs["shift_mu"])[0]
    lora = np.concatenate([mu[3 * D:], np.zeros(3 * P - LORA, np.float32)])
    conv = np.asarray(inputs["conv_w"])[0]
    one = lambda n: np.asarray(inputs[n]).reshape(-1)
    parts = [one("norm_mix_g"), mu[0:D], mu[D:2 * D], mu[2 * D:3 * D], lora, one("decay_w0"), one("iclr_a0"),
             one("k_k"), one("k_a"), one("r_k"), one("ln_x_g"), one("ln_x_b"), conv[0], conv[1], conv[2]]
    arrays["params"] = np.ascontiguousarray(np.concatenate([p.reshape(-1, P) for p in parts]).T)
    arrays["consts"] = constants()
    args = [nc.dram_tensor(f"in_{n}", a.shape, mybir.dt.from_np(a.dtype), kind="ExternalInput").ap()
            for n, a in arrays.items()]
    args.append(nc.dram_tensor("out_0", (1, T, D), F32, kind="ExternalOutput").ap())
    build(nc, *args)
    r = run_bass_kernel_spmd(nc, [{f"in_{n}": a for n, a in arrays.items()}], core_ids=[0])
    return r.results[0]["out_0"]
```
